# Optimizing a Trainium2 kernel written in Bass

```python
import jax, jax.numpy as jnp
from jax import lax
import numpy as np

D_MODEL = 1024
BATCH = 1
SEQ = 512
DEPTH = 2

CHUNK = 64
MEM_LEN = 256
HEAD_DIM = 64
EPS = 1e-6
X_HEADS = 4
X_WIDTH = X_HEADS * HEAD_DIM
TOK_WIDTH = D_MODEL - X_WIDTH
GMLP_BLOCK = 128
A_GROUPS = 4
A_GC = TOK_WIDTH // A_GROUPS
B_HEADS = TOK_WIDTH // HEAD_DIM
B_KV_HEADS = 3
B_GROUP = B_HEADS // B_KV_HEADS
KV_WIDTH = B_KV_HEADS * HEAD_DIM
WINDOW = 128
WINDOW_CHUNKS = WINDOW // CHUNK
ROPE_THETA = 500000.0
ROPE_DIM = HEAD_DIM // 4
D_FF = 4 * D_MODEL
N_A = (DEPTH + 1) // 2
N_B = DEPTH // 2

kernel_name = "hybrid_gmlp_swa_sink_memxattn_trunk"

def rms_norm(x, g):
    xf = x.astype(jnp.float32)
    y = xf * lax.rsqrt(jnp.mean(xf * xf, axis=-1, keepdims=True) + EPS)
    return (y * g.astype(jnp.float32)).astype(x.dtype)

def layer_norm(x, g, b):
    xf = x.astype(jnp.float32)
    mu = jnp.mean(xf, axis=-1, keepdims=True)
    xc = xf - mu
    y = xc * lax.rsqrt(jnp.mean(xc * xc, axis=-1, keepdims=True) + EPS)
    return (y * g.astype(jnp.float32) + b.astype(jnp.float32)).astype(x.dtype)

def partial_rope(x, positions):
    half = ROPE_DIM // 2
    inv_freq = jnp.power(ROPE_THETA, -jnp.arange(0, ROPE_DIM, 2, dtype=jnp.float32) / ROPE_DIM)
    ang = positions.astype(jnp.float32)[..., None] * inv_freq
    cos = jnp.cos(ang)[:, :, None, :]
    sin = jnp.sin(ang)[:, :, None, :]
    xf = x.astype(jnp.float32)
    x1 = xf[..., :half]
    x2 = xf[..., half:ROPE_DIM]
    rot = jnp.concatenate([x1 * cos - x2 * sin, x2 * cos + x1 * sin, xf[..., ROPE_DIM:]], axis=-1)
    return rot.astype(x.dtype)

def gmlp_spatial_gating(z_in, ln_g, ln_b, w_s, b_s):
    bsz, seq, _ = z_in.shape
    z = jax.nn.gelu(z_in, approximate=False)
    u = z[..., :TOK_WIDTH]
    v = layer_norm(z[..., TOK_WIDTH:], ln_g, ln_b)
    nblk = seq // GMLP_BLOCK
    v = v.reshape(bsz, nblk, GMLP_BLOCK, A_GROUPS, A_GC)
    u = u.reshape(bsz, nblk, GMLP_BLOCK, A_GROUPS, A_GC)
    c = jnp.arange(GMLP_BLOCK) // CHUNK
    allowed = c[None, :] <= c[:, None]
    w = jnp.where(allowed[None], w_s, jnp.zeros_like(w_s))
    sv = jnp.einsum('gts,bnsgc->bntgc', w, v) + b_s.T[:, :, None]
    return (u * sv).reshape(bsz, seq, TOK_WIDTH)

def shift_chunks(x, s):
    if s == 0:
        return x
    n_c = x.shape[1]
    pad = [(0, 0)] * x.ndim
    pad[1] = (s, 0)
    return jnp.pad(x, pad)[:, :n_c]

def swa_gqa_sinks(q, k, v, sinks):
    bsz, seq = q.shape[0], q.shape[1]
    n_c = seq // CHUNK
    qc = q.reshape(bsz, n_c, CHUNK, B_KV_HEADS, B_GROUP, HEAD_DIM)
    kc = k.reshape(bsz, n_c, CHUNK, B_KV_HEADS, HEAD_DIM)
    vc = v.reshape(bsz, n_c, CHUNK, B_KV_HEADS, HEAD_DIM)
    shifts = list(reversed(range(WINDOW_CHUNKS)))
    k_band = jnp.concatenate([shift_chunks(kc, s) for s in shifts], axis=2)
    v_band = jnp.concatenate([shift_chunks(vc, s) for s in shifts], axis=2)
    key_shift = (WINDOW_CHUNKS - 1) - jnp.arange(WINDOW) // CHUNK
    valid = jnp.arange(n_c)[:, None] >= key_shift[None, :]
    scores = jnp.einsum('bnqhgd,bnkhd->bnhgqk', qc, k_band).astype(jnp.float32) * (HEAD_DIM ** -0.5)
    scores = jnp.where(valid[None, :, None, None, None, :], scores, -jnp.inf)
    sink = sinks.astype(jnp.float32).reshape(1, 1, B_KV_HEADS, B_GROUP, 1, 1)
    m = jnp.maximum(jnp.max(scores, axis=-1, keepdims=True), sink)
    p = jnp.exp(scores - m)
    probs = (p / (jnp.sum(p, axis=-1, keepdims=True) + jnp.exp(sink - m))).astype(v.dtype)
    out = jnp.einsum('bnhgqk,bnkhd->bnqhgd', probs, v_band)
    return out.reshape(bsz, seq, B_HEADS * HEAD_DIM)

def memory_cross_attention(xq, mem, ln_mem, w_mem_kv, q_norm, k_norm):
    bsz, seq, _ = xq.shape
    q = rms_norm(xq.reshape(bsz, seq, X_HEADS, HEAD_DIM), q_norm)
    kv = rms_norm(mem, ln_mem) @ w_mem_kv
    k = rms_norm(kv[..., :X_WIDTH].reshape(bsz, -1, X_HEADS, HEAD_DIM), k_norm)
    v = kv[..., X_WIDTH:].reshape(bsz, -1, X_HEADS, HEAD_DIM)
    scores = jnp.einsum('bshd,bmhd->bhsm', q, k).astype(jnp.float32) * (HEAD_DIM ** -0.5)
    probs = jax.nn.softmax(scores, axis=-1).astype(v.dtype)
    out = jnp.einsum('bhsm,bmhd->bshd', probs, v)
    return out.reshape(bsz, seq, X_WIDTH)

def setup_inputs(seed: int = 0) -> dict:
    key = jax.random.key(seed)
    ks = jax.random.split(key, 24)
    f32 = jnp.float32
    nrm = lambda k, shape, scale: jax.random.normal(k, shape, f32) * scale
    gain = lambda k, shape: 1.0 + 0.02 * jax.random.normal(k, shape, f32)
    x = jax.random.normal(ks[0], (BATCH, SEQ, D_MODEL), f32)
    mem = jax.random.normal(ks[1], (BATCH, MEM_LEN, D_MODEL), f32)
    offset = jax.random.randint(ks[2], (BATCH, 1), 0, 64) * CHUNK
    positions = (offset + jnp.arange(SEQ, dtype=jnp.int32)[None, :]).astype(jnp.int32)
    return {
        "x": x,
        "mem": mem,
        "positions": positions,
        "ln_mix": gain(ks[3], (DEPTH, D_MODEL)),
        "ln_mem": gain(ks[4], (DEPTH, D_MODEL)),
        "w_mem_kv": nrm(ks[5], (DEPTH, D_MODEL, 2 * X_WIDTH), D_MODEL ** -0.5),
        "xq_norm": gain(ks[6], (DEPTH, HEAD_DIM)),
        "xk_norm": gain(ks[7], (DEPTH, HEAD_DIM)),
        "ln_mlp": gain(ks[8], (DEPTH, D_MODEL)),
        "w_up": nrm(ks[9], (DEPTH, D_MODEL, D_FF), D_MODEL ** -0.5),
        "w_down": nrm(ks[10], (DEPTH, D_FF, D_MODEL), D_FF ** -0.5),
        "a_w_in": nrm(ks[11], (N_A, D_MODEL, 2 * TOK_WIDTH + X_WIDTH), D_MODEL ** -0.5),
        "a_ln_g": gain(ks[12], (N_A, TOK_WIDTH)),
        "a_ln_b": nrm(ks[13], (N_A, TOK_WIDTH), 0.02),
        "a_w_s": nrm(ks[14], (N_A, A_GROUPS, GMLP_BLOCK, GMLP_BLOCK), 0.5 * GMLP_BLOCK ** -0.5),
        "a_b_s": gain(ks[15], (N_A, A_GROUPS, GMLP_BLOCK)),
        "a_w_out": nrm(ks[16], (N_A, TOK_WIDTH + X_WIDTH, D_MODEL), D_MODEL ** -0.5),
        "b_w_in": nrm(ks[17], (N_B, D_MODEL, TOK_WIDTH + 2 * KV_WIDTH + X_WIDTH), D_MODEL ** -0.5),
        "b_q_norm": gain(ks[18], (N_B, HEAD_DIM)),
        "b_k_norm": gain(ks[19], (N_B, HEAD_DIM)),
        "b_sinks": nrm(ks[20], (N_B, B_HEADS), 0.5),
        "b_w_out": nrm(ks[21], (N_B, TOK_WIDTH + X_WIDTH, D_MODEL), D_MODEL ** -0.5),
    }

def reference(x, mem, positions, ln_mix, ln_mem, w_mem_kv, xq_norm, xk_norm, ln_mlp, w_up, w_down,
              a_w_in, a_ln_g, a_ln_b, a_w_s, a_b_s, a_w_out,
              b_w_in, b_q_norm, b_k_norm, b_sinks, b_w_out):
    bsz, seq, _ = x.shape
    for i in range(DEPTH):
        j = i // 2
        h = rms_norm(x, ln_mix[i])
        if i % 2 == 0:
            proj = h @ a_w_in[j]
            tok = gmlp_spatial_gating(proj[..., :2 * TOK_WIDTH], a_ln_g[j], a_ln_b[j], a_w_s[j], a_b_s[j])
            xq = proj[..., 2 * TOK_WIDTH:]
            w_out = a_w_out[j]
        else:
            proj = h @ b_w_in[j]
            q = proj[..., :TOK_WIDTH].reshape(bsz, seq, B_HEADS, HEAD_DIM)
            k = proj[..., TOK_WIDTH:TOK_WIDTH + KV_WIDTH].reshape(bsz, seq, B_KV_HEADS, HEAD_DIM)
            v = proj[..., TOK_WIDTH + KV_WIDTH:TOK_WIDTH + 2 * KV_WIDTH].reshape(bsz, seq, B_KV_HEADS, HEAD_DIM)
            xq = proj[..., TOK_WIDTH + 2 * KV_WIDTH:]
            q = partial_rope(rms_norm(q, b_q_norm[j]), positions)
            k = partial_rope(rms_norm(k, b_k_norm[j]), positions)
            tok = swa_gqa_sinks(q, k, v, b_sinks[j])
            w_out = b_w_out[j]
        cross = memory_cross_attention(xq, mem, ln_mem[i], w_mem_kv[i], xq_norm[i], xk_norm[i])
        x = x + jnp.concatenate([tok, cross], axis=-1) @ w_out
        h = rms_norm(x, ln_mlp[i])
        x = x + jnp.square(jax.nn.relu(h @ w_up[i])) @ w_down[i]
    return x


_drawn_inputs = setup_inputs


def setup_inputs(seed=0):
    import zlib

    import numpy as np

    out = dict(_drawn_inputs(seed))
    spreads = {}
    factors = {'ln_mix': 4.149,
     'ln_mem': 8.0,
     'xq_norm': 8.0,
     'xk_norm': 8.0,
     'a_ln_g': 8.0,
     'a_ln_b': 8.0,
     'a_b_s': 5.319,
     'b_q_norm': 8.0,
     'b_k_norm': 8.0,
     'b_sinks': 8.0}
    for name, (base, spread) in spreads.items():
        noise = np.random.default_rng([zlib.crc32(name.encode()), seed]).standard_normal(out[name].shape)
        drawn = base * np.exp(spread * noise) if base else spread * noise
        out[name] = __import__('jax').numpy.asarray(drawn.astype(out[name].dtype))
    for name, factor in factors.items():
        out[name] = (out[name] * factor).astype(out[name].dtype)
    return out
```

```python
from contextlib import ExitStack

import numpy as np

import concourse.bass as bass
from concourse import mybir

F32 = mybir.dt.float32
F32R = mybir.dt.float32r
I32 = mybir.dt.int32
ALU = mybir.AluOpType
ACT = mybir.ActivationFunctionType
AX = mybir.AxisListType.X

P = 128
D = 1024
SEQ = 512
DEPTH = 2
MEM = 256
HD = 64
XH = 4
XW = XH * HD
TOK = D - XW
GROUPS = 4
GC = TOK // GROUPS
HEADS = TOK // HD
KVH = 3
CHUNK = 64
DFF = 4 * D
ROPE_DIM = HD // 4
ROPE_THETA = 500000.0
EPS = 1e-6
QK_SCALE = HD ** -0.5

KT = D // P
TT = SEQ // P
MT = MEM // P
TOKT = TOK // P
QUARTERS = DFF // D
SLOTS = 4
SWA_UNITS = KVH * TT
CROSS_UNITS = 2 * XH
SPATIAL_LAG = 3

H_MEMK = [0, 2]
H_MEMV = [4, 6]
H_L0 = 8
H_XQ = [H_L0, H_L0 + 2 + 2 * TOKT + KT + 2 * QUARTERS * KT]
H_V0 = H_XQ[0] + 2
H_U0 = H_V0 + TOKT
H_OUT0 = H_U0 + TOKT
H_MLP0 = H_OUT0 + KT
H_V1 = H_XQ[1] + 2
H_K1 = H_V1 + 2
H_Q1 = H_K1 + KVH
H_OUT1 = H_Q1 + TOKT
H_MLP1 = H_OUT1 + KT
H_OUT = [H_OUT0, H_OUT1]
H_MLP = [H_MLP0, H_MLP1]
HALVES = H_MLP1 + 2 * QUARTERS * KT
PAIRS = (HALVES + 1) // 2
assert H_XQ[1] == H_MLP0 + 2 * QUARTERS * KT and HALVES == 179
assert H_V1 % SLOTS <= SLOTS - 2 and all(h % 2 == 0 for h in (*H_MEMV, H_V0))


def plan_turns():
    order, used = [], {}

    def turn(name, *halves):
        for h in halves:
            used[h] = len(order)
        order.append(name)

    turn("MK0", 0, 1)
    turn("MK1", 2, 3)
    turn("MV0", 4, 5)
    turn("MS")
    turn("KN0")
    turn("KN1")
    turn("MV1", 6, 7)
    turn("NS0")
    turn("XQ0_0", H_XQ[0])
    turn("XQ0_1", H_XQ[0] + 1)
    for c in range(TOKT // 2):
        for t in range(TT):
            turn(f"V0_{c}_{t}", *((H_V0 + 2 * c, H_V0 + 2 * c + 1) if t == TT - 1 else ()))
            if (c, t) == (0, 0):
                turn("XS0")
                turn("RB0")
    for i in range(TOKT):
        turn(f"U{i}", H_U0 + i)
        if i >= SPATIAL_LAG:
            turn(f"SV{i - SPATIAL_LAG}")
    for i in range(TOKT - SPATIAL_LAG, TOKT):
        turn(f"SV{i}")
    for layer in range(DEPTH):
        if layer == 1:
            turn("XQ1_0", H_XQ[1])
            turn("XQ1_1", H_XQ[1] + 1)
            turn("NS2")
            for t in range(TT):
                turn(f"V1_{t}", *((H_V1, H_V1 + 1) if t == TT - 1 else ()))
                if t == 0:
                    turn("XS1")
            for g in range(KVH):
                turn(f"K{g}", H_K1 + g)
            turn("Q0", H_Q1)
            turn("KS")
            for g in range(KVH):
                turn(f"KR{g}")
            turn("QR0")
            for i in range(1, TOKT):
                turn(f"Q{i}", H_Q1 + i)
                if i <= KVH:
                    turn(f"KB{i - 1}")
                turn(f"QR{i}")
                if i % 2:
                    turn(f"QS{i // 2}")
            for w in range(SWA_UNITS):
                turn(f"SA{w}")
                turn(f"SB{w}")
        for d in range(KT):
            turn(f"OUT{layer}_{d}", H_OUT[layer] + d)
        h = H_MLP[layer]
        for t in range(KT):
            turn(f"UP{layer}_0_{t}", h + t)
            if t == 1:
                turn(f"NS{1 + 2 * layer}")
            if t == 3:
                turn(f"RB{1 + 2 * layer}")
        h += KT
        for q in range(QUARTERS):
            for t in range(KT):
                turn(f"DN{layer}_{q}_{t}", h)
                h += 1
            if q < QUARTERS - 1:
                for t in range(KT):
                    turn(f"UP{layer}_{q + 1}_{t}", h)
                    h += 1
    return {n: i for i, n in enumerate(order)}, used


TURN, USED_UP = plan_turns()
ACC = 4

C_MIX = [0, 8]
C_MLP = [16, 24]
C_MEM = [32, 40]
C_XQ = [48, 49]
C_XK = [50, 51]
C_BQ, C_BK = 52, 53
C_FREQ, C_EPS, C_EPS_SQ = 54, 55, 56
C_SINK = 57
N_COLS = C_SINK + HEADS


def high_bits(x, bits):
    e = np.floor(np.log2(abs(x))) + 1 - bits
    return float(np.floor(x / 2.0 ** e) * 2.0 ** e)


TWO_PI = 2 * np.pi
ROUND = float(1.5 * 2 ** 23)
FAR = TWO_PI * 2 ** 13
FAR_1 = high_bits(FAR, 8)
FAR_2 = high_bits(FAR - FAR_1, 8)
FAR_3 = float(FAR - FAR_1 - FAR_2)
PI_1 = high_bits(TWO_PI, 11)
PI_2 = high_bits(TWO_PI - PI_1, 11)
PI_3 = float(TWO_PI - PI_1 - PI_2)
BELOW_PI = 3.1415925
NO_KEY = -1e30


def build(nc, xT, memT, pos, W, cols_d, tabs_d, ln_d, bsx_d, wsT_d, out):
    with ExitStack() as ctx:
        def sb(name, shape, dt=F32):
            return ctx.enter_context(nc.sbuf_tensor(name, shape, dt))

        def psum(name, shape):
            return ctx.enter_context(nc.psum_tensor(name, shape, F32))

        def sem(name):
            return ctx.enter_context(nc.semaphore(name))

        x = sb("x", [P, KT, SEQ])
        xg_hi = sb("xg_hi", [P, KT, SEQ], F32R)
        xg_lo = sb("xg_lo", [P, KT, SEQ], F32R)
        hid_hi = sb("hid_hi", [P, KT, SEQ], F32R)
        hid_lo = sb("hid_lo", [P, KT, SEQ], F32R)
        w_raw = sb("w_raw", [P, SLOTS, KT * P])
        w_hi = sb("w_hi", [P, KT, SLOTS * P], F32R)
        w_lo = sb("w_lo", [P, KT, SLOTS * P], F32R)
        cols = sb("cols", [P, N_COLS])
        tabs = sb("tabs", [P, 3, P])
        ident, rotate, same_head = tabs[:, 0, :], tabs[:, 1, :], tabs[:, 2, :]
        blocks = same_head.rearrange("p (h n) -> p h n", h=2)[:, :, 0]
        ones = sb("ones", [P, P])
        eps_share = sb("eps_share", [P, P])
        kmem = sb("kmem", [P, DEPTH, 2, MEM])
        vmem = sb("vmem", [P, DEPTH, MT, XW])
        diag = sb("diag", [P, 2, 4, P])
        x_sq = sb("x_sq", [P, 2, SEQ])
        sq_sum = sb("sq_sum", [P, SEQ])
        r_row = sb("r_row", [P, SEQ])
        small = sb("small", [P, 512])
        probs = sb("probs", [P, 2, 512])
        probsT = sb("probsT", [P, 2, 512])
        relu, hid_sq, scaled = probs, probsT[:, 0, :], probsT[:, 1, :]
        qx = sb("qx", [P, 2, SEQ])
        qx_sq = sb("qx_sq", [P, 2, SEQ])
        gated = qx_sq
        work = sb("work", [P, 9728])

        at = [0]

        def carve(n, begin=None):
            if begin is not None:
                at[0] = begin
            at[0] += n
            return work[:, at[0] - n:at[0]]

        mem_in = carve(KT * MEM, 0).rearrange("p (k m) -> p k m", k=KT)
        mem_sq = carve(KT * MEM).rearrange("p (k m) -> p k m", k=KT)
        carve(2 * 512)
        k_sq0 = carve(2 * 512).rearrange("p (l n) -> p l n", l=2)
        v0 = carve(TT * TOK, 0).rearrange("p (t c) -> p t c", t=TT)
        u0 = carve(TOKT * SEQ).rearrange("p (i t) -> p i t", i=TOKT)
        ln_gb = carve(2 * TOK).rearrange("p (s c) -> p s c", s=2)
        bsx = carve(TOKT * P).rearrange("p (i t) -> p i t", i=TOKT)
        wsT = carve(GROUPS * P).rearrange("p (g t) -> p g t", g=GROUPS)
        cos_t = carve(SEQ, 0)
        sin_t = carve(SEQ)
        q1 = carve(TOKT * SEQ).rearrange("p (i t) -> p i t", i=TOKT)
        k1 = carve(KVH * SEQ).rearrange("p (i t) -> p i t", i=KVH)
        v1 = [carve(TT * KVH * HD).rearrange("p (t c) -> p t c", t=TT) for _ in range(2)]
        rot_s = carve(2 * SEQ).rearrange("p (b t) -> p b t", b=2)
        k_sq = carve(KVH * SEQ).rearrange("p (b t) -> p b t", b=KVH)
        ang, turns_n, far_t, pos_f = (q1[:, i, :] for i in range(4))
        pos_i = pos_f.bitcast(I32)

        sat = [0]

        def cols_of(n):
            sat[0] += n
            return small[:, sat[0] - n:sat[0]]

        mem_r = cols_of(MT)
        mem_ms = cols_of(MT)
        n_root = cols_of(TT)
        n_r = cols_of(TT)
        n_r2 = cols_of(TT)
        xs_a = cols_of(TT * XH)
        xs_b = cols_of(TT * XH)
        xs_r = cols_of(TT * XH)
        mx = cols_of(8)
        scaled_mx = cols_of(4)
        neg_m = cols_of(8)
        sums = cols_of(8)
        sink_e = cols_of(8)
        sink_d = cols_of(8)
        inv = cols_of(8)
        tot = cols_of(4)
        ln_st = cols_of(TT * 12)
        ln_mv = cols_of(TT * 2)
        ln_r = cols_of(TT)
        ln_root = cols_of(TT)
        ks_a = cols_of(TT * KVH)
        ks_b = cols_of(TT * KVH)
        ks_r = cols_of(TT * KVH)
        qs_a = cols_of(TT * HEADS)
        qs_b = cols_of(TT * HEADS)
        qs_r = cols_of(TT * HEADS)
        neg_sink = cols_of(HEADS)

        def v3(ap, a):
            return ap.rearrange("p (a b) -> p a b", a=a)

        acc = psum("acc", [P, ACC, 512])
        s_bank = psum("s_bank", [P, 2, 512])
        t_bank = psum("t_bank", [P, 512])
        o_bank = psum("o_bank", [P, 512])

        def swa_t(w):
            return s_bank[:, 0, :] if w % 2 else t_bank[:]

        def swa_o(m):
            return s_bank[:, 1, :] if m % 2 else o_bank[:]

        cols_in, tabs_in, ln_in, pos_in, v_shifted, stored = (
            sem(n) for n in ("cols_in", "tabs_in", "ln_in", "pos_in", "v_shifted", "stored"))
        mem_loaded = [sem(f"mem_loaded{i}") for i in range(4)]
        x_loaded = [sem(f"x_loaded{i}") for i in range(4)]
        first_loaded = [sem(f"first_loaded{i}") for i in range(SLOTS)]
        w_loaded = [sem(f"w_loaded{i}") for i in range(2)]
        w_hi_done, w_ready = sem("w_hi_done"), sem("w_ready")
        ones_set, eps_set, wsT_masked, v_zeroed = sem("ones_set"), sem("eps_set"), sem("wsT_masked"), sem("v_zeroed")
        turn_done = sem("turn_done")
        acc_free = [sem(f"acc_free{i}") for i in range(ACC)]
        mem_hi, mem_lo, memsq_done, memsq_added, kmem_done = (
            sem(n) for n in ("mem_hi", "mem_lo", "memsq_done", "memsq_added", "kmem_done"))
        xg_hi_done, xg_lo_done, x_squared, sq_added = (
            sem(n) for n in ("xg_hi_done", "xg_lo_done", "x_squared", "sq_added"))
        root_done = sem("root_done")
        mem_r_ready, n2_ready = sem("mem_r_ready"), sem("n2_ready")
        diag_done = sem("diag_done")
        s_done, t_done, o_done = sem("s_done"), sem("t_done"), sem("o_done")
        neg_m_done, exp_done, sink_exp = sem("neg_m_done"), sem("exp_done"), sem("sink_exp")
        inv_done, pn_cross, pn_swa = sem("inv_done"), sem("pn_cross"), sem("pn_swa")
        pT_act, pT_dve = sem("pT_act"), sem("pT_dve")
        hid_hi_done, hid_done = sem("hid_hi_done"), sem("hid_done")
        v0_gelu, ln_stats, v0_normed, v0_done = (sem(n) for n in ("v0_gelu", "ln_stats", "v0_normed", "v0_done"))
        u_done, gated_done = sem("u_done"), sem("gated_done")
        sin_arg, trig_done = sem("sin_arg"), sem("trig_done")
        rot_cos, q_rot = sem("rot_cos"), sem("q_rot")
        hid_squared, x_updated = sem("hid_squared"), sem("x_updated")
        dve_step = sem("dve_step")

        block = ctx.enter_context(nc.Block())

        HID_L = KT + QUARTERS * KT
        X_L = QUARTERS * KT
        ROOT = {n: i + 1 for i, n in enumerate(["xs0", "ln", "xs1", "ks", "qs"])}
        DIAG_TURN = {"n0": "RB0", "n1": "RB1", "kb0": "KB0", "kb1": "KB1", "kb2": "KB2", "n3": "RB3"}
        DIAG = {n: i + 1 for i, n in enumerate(DIAG_TURN)}

        def bank(t):
            return t % ACC

        def acc_of(name):
            return acc[:, bank(TURN[name]), :]

        def release(ins, name):
            ins.then_inc(acc_free[bank(TURN[name])], 1)

        def wait_read(eng, name):
            eng.wait_ge(acc_free[bank(TURN[name])], TURN[name] // ACC + 1)

        def slot(h, n=1):
            s = h % SLOTS
            return slice(s * P, (s + n) * P)

        @block.sync
        def _(sp):
            def load(pair, free, sems):
                sp.wait_ge(w_ready, free)
                sp.dma_start(w_raw[:, 2 * sems:2 * sems + 2, :].rearrange("p s n -> p (s n)"),
                             W[bass.ds(pair, 1), :, :].rearrange("o p n -> p (o n)")
                             if not isinstance(pair, int) else W[pair, :, :]).then_inc(w_loaded[sems], 16)

            def first(h):
                sp.dma_start(w_raw[:, h, :], W[h // 2, :, (h % 2) * KT * P:(h % 2 + 1) * KT * P]).then_inc(
                    first_loaded[h], 16)

            def load_mem(i):
                sp.dma_start(mem_in[:, 2 * i:2 * i + 2, :], memT[:, 2 * i:2 * i + 2, :]).then_inc(mem_loaded[i], 16)

            first(0)
            load_mem(0)
            first(1)
            for i in range(1, 4):
                load_mem(i)
            first(2)
            first(3)
            load(2, 2, 0)
            for i in range(4):
                sp.dma_start(x[:, 2 * i:2 * i + 2, :], xT[:, 2 * i:2 * i + 2, :]).then_inc(x_loaded[i], 16)
            load(3, 4, 1)
            assert PAIRS % 2 == 0
            with sp.Fori(2, PAIRS // 2) as i:
                for s in range(2):
                    load(2 * i + s, 4 * i + (2 * s - 2), s)
            for k in range(KT):
                sp.wait_ge(x_updated, DEPTH * X_L - KT + k + 1)
                sp.dma_start(out[:, k, :], x[:, k, :]).then_inc(stored, 16)
            sp.wait_ge(stored, 16 * KT)

        @block.gpsimd
        def _(pool):
            pool.memset(ones[:], 1.0).then_inc(ones_set, 1)
            pool.memset(eps_share[:], EPS * HD / D).then_inc(eps_set, 1)

            def split(h, done):
                pool.wait_ge(w_hi_done, done)
                o = w_lo[:, :, slot(h)]
                pool.tensor_tensor(o, w_raw[:, h % SLOTS, :].rearrange("p (k n) -> p k n", k=KT),
                                   w_hi[:, :, slot(h)].bitcast(F32), ALU.subtract).then_inc(w_ready, 1)

            def splits(a, b):
                for h in range(a, b):
                    split(h, h + 1)

            def add_square(n, k):
                c = KT * n + k
                pool.wait_ge(x_squared, c + 1)
                if k == 0:
                    pool.wait_ge(turn_done, TURN[f"NS{n - 1}"] + 1)
                    pool.tensor_copy(sq_sum[:], x_sq[:, 0, :]).then_inc(sq_added, 1)
                else:
                    pool.wait_ge(sq_added, c)
                    pool.tensor_tensor(sq_sum[:], sq_sum[:], x_sq[:, k % 2, :], ALU.add).then_inc(sq_added, 1)

            def mlp(layer):
                h0 = H_MLP[layer]
                ahead = SLOTS
                splits(h0 + ahead, h0 + KT + ahead)
                body = h0 + KT + ahead
                with pool.Fori(0, QUARTERS - 1) as q:
                    for j in range(2 * KT):
                        split(body + j, q * (2 * KT) + (body + j + 1))

            def mlp_end(layer):
                body = H_MLP[layer] + KT + SLOTS + 2 * KT * (QUARTERS - 1)
                for t in range(KT):
                    if body + t < HALVES:
                        split(body + t, body + t + 1)
                    if layer < DEPTH - 1 and t >= 1:
                        add_square(2 * (layer + 1), t - 1)
                if layer < DEPTH - 1:
                    add_square(2 * (layer + 1), KT - 1)

            pool.wait_ge(w_ready, 1)
            splits(1, H_U0 + SLOTS + 1)
            for t in range(TT - 1):
                pool.wait_ge(v0_normed, t + 1)
                pool.tensor_tensor(v0[:, t, :], v0[:, t, :], ln_gb[:, 1, :], ALU.add).then_inc(v0_done, 1)

            def gate(i):
                wait_read(pool, f"SV{i}")
                pool.wait_ge(u_done, i + 1)
                pool.tensor_tensor(gated[:, i % 2, :], gated[:, i % 2, :], u0[:, i, :],
                                   ALU.mult).then_inc(gated_done, 1)

            for i in range(1, TOKT):
                split(H_U0 + SLOTS + i, H_U0 + SLOTS + i + 1)
                if i >= SPATIAL_LAG:
                    gate(i - SPATIAL_LAG)
            for i in range(TOKT - SPATIAL_LAG, TOKT):
                gate(i)
            for layer in range(DEPTH):
                if layer == 1:
                    def cos_part(tile, name):
                        pool.wait_ge(turn_done, TURN[name] + 1)
                        pool.tensor_tensor(tile, tile, cos_t, ALU.mult).then_inc(rot_cos, 1)

                    splits(H_XQ[1] + SLOTS, H_Q1 + 2)
                    pool.wait_ge(trig_done, 2)
                    for g in range(KVH):
                        cos_part(k1[:, g, :], f"KR{g}")
                    split(H_Q1 + 2, H_Q1 + 3)
                    split(H_Q1 + 3, H_Q1 + 4)
                    cos_part(q1[:, 0, :], "QR0")
                    for i in range(1, TOKT):
                        split(H_Q1 + 3 + i, H_Q1 + 4 + i)
                        cos_part(q1[:, i, :], f"QR{i}")
                    split(H_OUT1 + 3, H_OUT1 + 4)
                    for w in range(SWA_UNITS):
                        pool.wait_ge(inv_done, w + 1)
                        pool.tensor_tensor(v3(probs[:, w % 2, :], 4), v3(probs[:, w % 2, :], 4),
                                           inv[:, 4 * (w % 2):4 * (w % 2) + 4].unsqueeze(2).broadcast_to([P, 4, P]),
                                           ALU.mult).then_inc(pn_swa, 1)
                for d in range(KT):
                    split(H_OUT[layer] + SLOTS + d, H_OUT[layer] + SLOTS + d + 1)
                    if d >= 1:
                        add_square(1 + 2 * layer, d - 1)
                add_square(1 + 2 * layer, KT - 1)
                mlp(layer)
                mlp_end(layer)

        @block.scalar
        def _(act):
            act.dma_start(cols[:], cols_d).then_inc(cols_in, 16)
            eps = cols[:, C_EPS:C_EPS + 1]

            def split_hi(h, loaded, s):
                if isinstance(h, int) and h < SLOTS:
                    act.wait_ge(first_loaded[h], 16)
                else:
                    act.wait_ge(w_loaded[s // 2], loaded)
                act.activation(w_hi[:, :, slot(h)], w_raw[:, s, :].rearrange("p (k n) -> p k n", k=KT),
                               ACT.Copy).then_inc(w_hi_done, 1)

            nexth = [0]

            def weights(after=None, end=HALVES):
                while nexth[0] < end:
                    h = nexth[0]
                    if h >= SLOTS:
                        if after is None or USED_UP[h - SLOTS] > TURN[after]:
                            return
                        act.wait_ge(turn_done, USED_UP[h - SLOTS] + 1)
                    split_hi(h, 16 * (h // SLOTS), h % SLOTS)
                    nexth[0] += 1

            def ready(name):
                act.wait_ge(turn_done, TURN[name] + 1)
                return acc_of(name)

            def root(name, out_, in_):
                act.activation(out_, in_, ACT.Sqrt, bias=eps, scale=1.0 / HD).then_inc(root_done, 1)

            def root_of_turn(name, out_, n):
                release(act.activation(out_, ready(name)[:, 0:n], ACT.Sqrt, bias=eps, scale=1.0 / D), name)

            def prepare_hi(n, k, gain):
                act.activation(xg_hi[:, k, :], x[:, k, :], ACT.Identity,
                               scale=cols[:, gain + k:gain + k + 1]).then_inc(xg_hi_done, 1)
                if KT * n + k >= 2:
                    act.wait_ge(sq_added, KT * n + k - 1)
                act.activation(x_sq[:, k % 2, :], x[:, k, :], ACT.Square).then_inc(x_squared, 1)

            def q_evacuate(name, dst, gain, sq):
                src = ready(name)
                act.activation(dst, src, ACT.Identity, scale=cols[:, gain:gain + 1])
                release(act.activation(sq, src, ACT.Square), name)

            def cross_exp(layer, u):
                U = CROSS_UNITS * layer + u
                i, th, h2 = u // 4, (u // 2) % 2, u % 2
                b = U % 2
                act.wait_ge(neg_m_done, U + 1)
                if U >= 2:
                    act.wait_ge(t_done, U - 1)
                for t2 in range(2):
                    t = 2 * th + t2
                    ins = act.activation(probs[:, b, t2 * MEM:(t2 + 1) * MEM], s_bank[:, h2, t2 * MEM:(t2 + 1) * MEM],
                                         ACT.Exp, bias=neg_m[:, 4 * b + t2:4 * b + t2 + 1],
                                         scale=xs_r[:, t * XH + 2 * i + h2:t * XH + 2 * i + h2 + 1],
                                         accum_out=sums[:, 4 * b + t2:4 * b + t2 + 1])
                ins.then_inc(exp_done, 1)

            def cross_pT(layer, u):
                U = CROSS_UNITS * layer + u
                act.wait_ge(t_done, U + 1)
                if U >= 2:
                    act.wait_ge(o_done, U - 1)
                act.activation(probsT[:, U % 2, :], t_bank[:], ACT.Copy).then_inc(pT_act, 1)

            def cross_out(layer, i):
                act.wait_ge(o_done, CROSS_UNITS * layer + 4 * i + 4)
                if layer == 0:
                    act.wait_ge(turn_done, TURN["MV1"] + 1)
                act.activation(hid_hi[:, TOKT + i, :], o_bank[:], ACT.Copy).then_inc(hid_hi_done, 1)

            def cross_step(layer, s):
                if s < CROSS_UNITS:
                    cross_exp(layer, s)
                if 2 <= s < CROSS_UNITS + 2:
                    cross_pT(layer, s - 2)
                if s == 6 or s == 10:
                    cross_out(layer, (s - 6) // 4)

            def mlp_up(layer, q, t, tn, b, n_read):
                act.wait_ge(turn_done, tn + 1)
                act.wait_ge(hid_done, (q * KT) + (HID_L * layer + KT + t - 1))
                act.activation(relu[:, t % 2, :], acc[:, b, :], ACT.Relu).then_inc(acc_free[b], 1)
                act.wait_ge(acc_free[b], n_read)
                act.activation(hid_hi[:, t, :], relu[:, t % 2, :], ACT.Square).then_inc(hid_hi_done, 1)

            weights(None, 3)
            act.wait_ge(cols_in, 16)
            for k in range(KT):
                act.wait_ge(mem_loaded[k // 2], 16)
                act.activation(hid_hi[:, k, MEM:2 * MEM], mem_in[:, k, :], ACT.Identity,
                               scale=cols[:, C_MEM[1] + k:C_MEM[1] + k + 1]).then_inc(mem_hi, 1)
                if k == KT // 2 - 1:
                    weights()
            act.dma_start(tabs[:], tabs_d).then_inc(tabs_in, 16)
            for i in range(4):
                act.activation(mem_sq[:, 2 * i:2 * i + 2, :], mem_in[:, 2 * i:2 * i + 2, :],
                               ACT.Square).then_inc(memsq_done, 1)
            for l in range(DEPTH):
                src = ready(f"MK{l}")
                act.activation(kmem[:, l, :, :], v3(src, 2), ACT.Identity,
                               scale=cols[:, C_XK[l]:C_XK[l] + 1])
                release(act.activation(k_sq0[:, l, :], src, ACT.Square), f"MK{l}")
                weights(f"MK{l}")
                for k in range(l * KT // 2, (l + 1) * KT // 2):
                    if k % 2 == 0:
                        act.wait_ge(x_loaded[k // 2], 16)
                    prepare_hi(0, k, C_MIX[0])
            act.dma_start(ln_gb, ln_d.unsqueeze(0).broadcast_to([P, 2, TOK])).then_inc(ln_in, 16)
            act.dma_start(bsx, bsx_d).then_inc(ln_in, 16)
            act.dma_start(wsT, wsT_d).then_inc(ln_in, 16)

            def mem_values(l):
                src = ready(f"MV{l}")
                act.wait_ge(mem_r_ready, 1)
                for m in range(MT):
                    ins = act.activation(vmem[:, l, m, :], src[:, m * XW:(m + 1) * XW], ACT.Identity,
                                         scale=mem_r[:, m:m + 1])
                release(ins, f"MV{l}")
                weights(f"MV{l}")

            root_of_turn("MS", mem_ms, MT)
            mem_values(0)
            for l in range(DEPTH):
                name = f"KN{l}"
                release(act.activation(k_sq0[:, l, :], ready(name), ACT.Sqrt, bias=cols[:, C_EPS_SQ:C_EPS_SQ + 1],
                                       scale=1.0 / HD), name)
            mem_values(1)

            root_of_turn("NS0", n_root, TT)
            for i in range(2):
                q_evacuate(f"XQ0_{i}", qx[:, i, :], C_XQ[0], qx_sq[:, i, :])
                weights(f"XQ0_{i}")
            wait_read(act, "XS0")
            root("xs0", xs_b, xs_a)
            release(act.activation(r_row[:], ready("RB0"), ACT.Copy), "RB0")
            s = 0
            for c in range(TOKT // 2):
                for t in range(TT):
                    if s < CROSS_UNITS + 3:
                        cross_step(0, s)
                    s += 1
                    weights(f"V0_{c}_{t}")
            for t in range(TT):
                wait_read(act, f"V0_{TOKT // 2 - 1}_{t}")
                act.activation(v0[:, t, :], v0[:, t, :], ACT.Gelu).then_inc(v0_gelu, 1)
            act.wait_ge(ln_stats, 1)
            act.activation(ln_root, ln_mv.rearrange("p (t s) -> p t s", s=2)[:, :, 1], ACT.Sqrt,
                           bias=eps).then_inc(root_done, 1)

            def u_gelu(i):
                wait_read(act, f"U{i}")
                act.activation(u0[:, i, :], u0[:, i, :], ACT.Gelu).then_inc(u_done, 1)

            def gate_hi(i):
                act.wait_ge(gated_done, i + 1)
                act.activation(hid_hi[:, i, :], gated[:, i % 2, :], ACT.Copy).then_inc(hid_hi_done, 1)

            for i in range(TOKT):
                weights(f"U{i}")
                u_gelu(i)
                if i >= SPATIAL_LAG:
                    gate_hi(i - SPATIAL_LAG)
            for i in range(TOKT - SPATIAL_LAG, TOKT):
                gate_hi(i)

            for layer in range(DEPTH):
                if layer == 1:
                    for i in range(2):
                        q_evacuate(f"XQ1_{i}", qx[:, i, :], C_XQ[1], qx_sq[:, i, :])
                        weights(f"XQ1_{i}")
                    root_of_turn("NS2", n_root, TT)
                    act.wait_ge(n2_ready, 1)
                    for t in range(TT):
                        release(act.activation(v1[1][:, t, :], ready(f"V1_{t}")[:, 0:KVH * HD], ACT.Identity,
                                               scale=n_r[:, t:t + 1]), f"V1_{t}")
                        weights(f"V1_{t}")
                    for t in range(TT):
                        wait_read(act, f"V1_{t}")
                    act.dma_start(v1[0][CHUNK:P, :, :], v1[1][0:CHUNK, :, :]).then_inc(v_shifted, 16)
                    act.dma_start(v1[0][0:CHUNK, 1:TT, :], v1[1][CHUNK:P, 0:TT - 1, :]).then_inc(v_shifted, 16)
                    wait_read(act, "XS1")
                    root("xs1", xs_b, xs_a)
                    for g in range(KVH):
                        q_evacuate(f"K{g}", k1[:, g, :], C_BK, k_sq[:, g, :])
                        weights(f"K{g}")
                    act.wait_ge(turn_done, TURN["XS1"] + 1)
                    q_evacuate("Q0", q1[:, 0, :], C_BQ, qx_sq[:, 0, :])
                    weights("Q0")
                    wait_read(act, "KS")
                    root("ks", ks_b, ks_a)
                    cross_step(1, 0)
                    cross_step(1, 1)
                    for i in range(1, TOKT):
                        if i >= 2:
                            act.wait_ge(turn_done, TURN[f"QS{i // 2 - 1}"] + 1)
                        q_evacuate(f"Q{i}", q1[:, i, :], C_BQ, qx_sq[:, i % 2, :])
                        weights(f"Q{i}")
                        cross_step(1, 2 * i)
                        cross_step(1, 2 * i + 1)
                    wait_read(act, f"QS{KVH - 1}")
                    root("qs", qs_b, qs_a)

                    def swa_exp(w):
                        g, j = divmod(w, TT)
                        b = w % 2
                        act.wait_ge(neg_m_done, 2 * CROSS_UNITS + w + 1)
                        if w >= 2:
                            act.wait_ge(t_done, 2 * CROSS_UNITS + w - 1)
                        for e in range(4):
                            name = ("SA", "SB")[e // 2] + str(w)
                            c = j * HEADS + 4 * g + e
                            ins = act.activation(probs[:, b, e * P:(e + 1) * P],
                                                 acc_of(name)[:, (e % 2) * P:(e % 2 + 1) * P], ACT.Exp,
                                                 bias=neg_m[:, 4 * b + e:4 * b + e + 1], scale=qs_r[:, c:c + 1],
                                                 accum_out=sums[:, 4 * b + e:4 * b + e + 1])
                            if e % 2:
                                release(ins, name)
                        act.activation(sink_e[:, 4 * b:4 * b + 4], sink_d[:, 4 * b:4 * b + 4],
                                       ACT.Exp).then_inc(sink_exp, 1)

                    def swa_out(m):
                        g, jj = divmod(m, 2)
                        act.wait_ge(o_done, 2 * CROSS_UNITS + 2 * m + 2)
                        act.activation(
                            hid_hi[:, 2 * g:2 * g + 2, 2 * jj * P:(2 * jj + 2) * P].rearrange("p i (j t) -> p j i t", j=2),
                            swa_o(m).rearrange("p (j i t) -> p j i t", j=2, i=2), ACT.Copy).then_inc(hid_hi_done, 1)

                    for w in range(SWA_UNITS):
                        swa_exp(w)
                        if w >= 4 and w % 2 == 0:
                            swa_out((w - 4) // 2)
                    for m in range(SWA_UNITS // 2 - 2, SWA_UNITS // 2):
                        swa_out(m)

                for d in range(KT):
                    weights(f"OUT{layer}_{d}")
                    wait_read(act, f"OUT{layer}_{d}")
                    prepare_hi(1 + 2 * layer, d, C_MLP[layer])
                if layer == 0:
                    act.dma_start(pos_i, pos.unsqueeze(0).broadcast_to([P, SEQ])).then_inc(pos_in, 16)
                for t in range(KT):
                    name = f"UP{layer}_0_{t}"
                    tn = TURN[name]
                    mlp_up(layer, 0, t, tn, bank(tn), tn // ACC + 1)
                    weights(name)
                    if t == 1:
                        root_of_turn(f"NS{1 + 2 * layer}", n_root, TT)
                    if t == 4:
                        name = f"RB{1 + 2 * layer}"
                        release(act.activation(r_row[:], ready(name), ACT.Copy), name)
                body = TURN[f"DN{layer}_0_0"]
                hb = H_MLP[layer] + KT + SLOTS
                assert nexth[0] == hb
                with act.Fori(0, QUARTERS - 1) as q:
                    for j in range(2 * KT):
                        tn = q * (2 * KT) + (body + j)
                        if j < KT:
                            act.wait_ge(turn_done, tn + 1)
                        else:
                            mlp_up(layer, q + 1, j - KT, tn, bank(body + j),
                                   q * (2 * KT // ACC) + ((body + j) // ACC + 1))
                        h = hb + j
                        split_hi(h, q * (2 * KT // SLOTS * 16) + 16 * (h // SLOTS), h % SLOTS)
                nexth[0] = hb + 2 * KT * (QUARTERS - 1)
                if layer == 0:
                    for n, t in enumerate((sin_t, cos_t)):
                        act.wait_ge(sin_arg, n + 1)
                        act.activation(t, t, ACT.Sin).then_inc(trig_done, 1)
                for t in range(KT):
                    weights(f"DN{layer}_{QUARTERS - 1}_{t}")
                    if layer < DEPTH - 1:
                        act.wait_ge(x_updated, X_L * (layer + 1) - KT + t + 1)
                        prepare_hi(2 * (layer + 1), t, C_MIX[layer + 1])

        @block.vector
        def _(dve):
            steps = [0]

            def link(ins):
                steps[0] += 1
                ins.then_inc(dve_step, 1)
                dve.wait_ge(dve_step, steps[0])

            def ready(name):
                dve.wait_ge(turn_done, TURN[name] + 1)
                return acc_of(name)

            def along(ap, n):
                return ap.unsqueeze(2).broadcast_to([P, ap.shape[1], n])

            def prepare_lo(n, k, gain):
                dve.wait_ge(xg_hi_done, KT * n + k + 1)
                dve.scalar_tensor_tensor(xg_lo[:, k, :], x[:, k, :], cols[:, gain + k:gain + k + 1],
                                         xg_hi[:, k, :].bitcast(F32), ALU.mult,
                                         ALU.subtract).then_inc(xg_lo_done, 1)

            def norm_factors(name):
                wait_read(dve, name)
                link(dve.reciprocal(n_r, n_root))
                link(dve.tensor_tensor(n_r2, n_r, n_r, ALU.mult))

            def diagonal(name, factors):
                n = DIAG[name]
                if n > 2:
                    dve.wait_ge(turn_done, TURN[DIAG_TURN[list(DIAG)[n - 3]]] + 1)
                dve.tensor_tensor(diag[:, n % 2, :, :], ident.unsqueeze(1).broadcast_to([P, 4, P]),
                                  along(factors, P), ALU.mult).then_inc(diag_done, 1)

            def cross_factors(layer):
                name = f"XS{layer}"
                release(dve.tensor_tensor(v3(xs_a, TT), v3(ready(name)[:, 0:TT * XH], TT), along(n_r2, XH),
                                          ALU.mult), name)
                dve.wait_ge(root_done, ROOT[f"xs{layer}"])
                link(dve.reciprocal(xs_b, xs_b))
                link(dve.scalar_tensor_tensor(v3(xs_r, TT), v3(xs_b, TT), QK_SCALE, along(n_r, XH),
                                              ALU.mult, ALU.mult))

            def cross_max(layer, u):
                U = CROSS_UNITS * layer + u
                i, th, h2 = u // 4, (u // 2) % 2, u % 2
                b = U % 2
                dve.wait_ge(s_done, U + 1)
                link(dve.tensor_reduce(mx[:, 4 * b:4 * b + 2], v3(s_bank[:, h2, :], 2), AX, ALU.max))
                dve.scalar_tensor_tensor(neg_m[:, 4 * b:4 * b + 2], mx[:, 4 * b:4 * b + 2], -1.0,
                                         v3(xs_r, TT)[:, 2 * th:2 * th + 2, 2 * i + h2],
                                         ALU.mult, ALU.mult).then_inc(neg_m_done, 1)

            def cross_norm(layer, u):
                U = CROSS_UNITS * layer + u
                b = U % 2
                dve.wait_ge(exp_done, U + 1)
                link(dve.reciprocal(inv[:, 4 * b:4 * b + 2], sums[:, 4 * b:4 * b + 2]))
                dve.tensor_tensor(v3(probs[:, b, :], 2), v3(probs[:, b, :], 2), along(inv[:, 4 * b:4 * b + 2], MEM),
                                  ALU.mult).then_inc(pn_cross, 1)

            def cross_step(layer, s):
                if s < CROSS_UNITS:
                    cross_max(layer, s)
                if 1 <= s <= CROSS_UNITS:
                    cross_norm(layer, s - 1)
                if s == 6 or s == 10:
                    i = (s - 6) // 4
                    dve.wait_ge(hid_hi_done, HID_L * layer + i + 1)
                    dve.tensor_tensor(hid_lo[:, TOKT + i, :], o_bank[:], hid_hi[:, TOKT + i, :].bitcast(F32),
                                      ALU.subtract).then_inc(hid_done, 1)

            def out_update(layer, d):
                name = f"OUT{layer}_{d}"
                release(dve.tensor_tensor(x[:, d, :], ready(name), x[:, d, :], ALU.add), name)
                wait_read(dve, name)

            def mlp_up(layer, q, t, b, n_read):
                dve.wait_ge(acc_free[b], n_read)
                dve.wait_ge(hid_done, (q * KT) + (HID_L * layer + KT + t))
                dve.tensor_tensor(hid_sq, relu[:, t % 2, :], relu[:, t % 2, :], ALU.mult).then_inc(hid_squared, 1)
                dve.wait_ge(hid_squared, (q * KT) + (layer * QUARTERS * KT + t + 1))
                dve.wait_ge(hid_hi_done, (q * KT) + (HID_L * layer + KT + t + 1))
                dve.tensor_tensor(hid_lo[:, t, :], hid_sq, hid_hi[:, t, :].bitcast(F32),
                                  ALU.subtract).then_inc(hid_done, 1)

            def mlp_down(layer, q, t, tn, b, n_read):
                dve.wait_ge(turn_done, tn + 1)
                if t:
                    dve.wait_ge(x_updated, (q * KT) + (X_L * layer + t))
                dve.tensor_tensor(scaled, acc[:, b, :], r_row[:], ALU.mult).then_inc(acc_free[b], 1)
                dve.wait_ge(acc_free[b], n_read)
                dve.tensor_tensor(x[:, t, :], x[:, t, :], scaled, ALU.add).then_inc(x_updated, 1)
                if t == KT - 1:
                    dve.wait_ge(x_updated, (q * KT) + (X_L * layer + KT))

            dve.wait_ge(cols_in, 16)

            def mem_split(l, k):
                gain = cols[:, C_MEM[l] + k:C_MEM[l] + k + 1]
                hi = hid_hi[:, k, l * MEM:(l + 1) * MEM]
                dve.wait_ge(mem_loaded[k // 2], 16)
                if l == 0:
                    link(dve.tensor_scalar(hi, mem_in[:, k, :], gain, None, ALU.mult))
                else:
                    dve.wait_ge(mem_hi, k + 1)
                dve.scalar_tensor_tensor(hid_lo[:, k, l * MEM:(l + 1) * MEM], mem_in[:, k, :], gain,
                                         hi.bitcast(F32), ALU.mult, ALU.subtract).then_inc(mem_lo, 1)

            mem_split(0, 0)
            mem_split(0, 1)
            dve.wait_ge(w_hi_done, 1)
            dve.tensor_tensor(w_lo[:, :, slot(0)], w_raw[:, 0, :].rearrange("p (k n) -> p k n", k=KT),
                              w_hi[:, :, slot(0)].bitcast(F32), ALU.subtract).then_inc(w_ready, 1)
            for k in range(2, KT):
                mem_split(0, k)
            for k in range(KT):
                mem_split(1, k)
            n = KT // 2
            dve.wait_ge(memsq_done, 4)
            while n:
                ins = dve.tensor_tensor(mem_sq[:, 0:n, :], mem_sq[:, 0:n, :], mem_sq[:, n:2 * n, :], ALU.add)
                if n > 1:
                    link(ins)
                n //= 2
            ins.then_inc(memsq_added, 1)
            for k in range(KT):
                prepare_lo(0, k, C_MIX[0])
                dve.wait_ge(x_squared, k + 1)
                if k:
                    dve.wait_ge(sq_added, k)
                    dve.tensor_tensor(sq_sum[:], sq_sum[:], x_sq[:, k % 2, :], ALU.add).then_inc(sq_added, 1)
                else:
                    dve.tensor_copy(sq_sum[:], x_sq[:, 0, :]).then_inc(sq_added, 1)
            wait_read(dve, "MS")
            link(dve.reciprocal(mem_r, mem_ms))
            link(dve.tensor_copy(neg_sink, cols[:, C_SINK:C_SINK + HEADS]))
            dve.tensor_scalar(neg_sink, neg_sink, -1.0, None, ALU.mult).then_inc(mem_r_ready, 1)
            for l in range(DEPTH):
                wait_read(dve, f"KN{l}")
                link(dve.reciprocal(k_sq0[:, l, :], k_sq0[:, l, :]))
                dve.tensor_tensor(kmem[:, l, :, :], kmem[:, l, :, :], v3(k_sq0[:, l, :], 2),
                                  ALU.mult).then_inc(kmem_done, 1)

            norm_factors("NS0")
            step = 0
            for c in range(TOKT // 2):
                for t in range(TT):
                    name = f"V0_{c}_{t}"
                    release(dve.tensor_scalar(v0[:, t, 2 * c * P:2 * (c + 1) * P], ready(name)[:, 0:2 * P],
                                              n_r[:, t:t + 1], None, ALU.mult), name)
                    if (c, t) == (0, 0):
                        diagonal("n0", n_r)
                        cross_factors(0)
                    if step < CROSS_UNITS + 3:
                        cross_step(0, step)
                    step += 1
            for t in range(TT):
                dve.wait_ge(v0_gelu, t + 1)
                for e in range(2):
                    ins = dve.bn_stats(ln_st[:, 12 * t + 6 * e:12 * t + 6 * e + 6], v0[:, t, e * TOK // 2:(e + 1) * TOK // 2])
                link(ins)
                ins = dve.bn_aggr(ln_mv[:, 2 * t:2 * t + 2], ln_st[:, 12 * t:12 * t + 12])
            ins.then_inc(ln_stats, 1)
            dve.wait_ge(root_done, ROOT["ln"])
            link(dve.reciprocal(ln_r, ln_root))
            dve.wait_ge(ln_in, 48)
            dve.memset(wsT[CHUNK:P, :, 0:CHUNK], 0.0).then_inc(wsT_masked, 1)
            def u_scale(i):
                release(dve.tensor_tensor(u0[:, i, :], ready(f"U{i}"), r_row[:], ALU.mult), f"U{i}")

            wait_read(dve, "RB0")
            for t in range(TT):
                if t % 2 == 0:
                    u_scale(t // 2)
                link(dve.tensor_scalar(v0[:, t, :], v0[:, t, :], ln_mv[:, 2 * t:2 * t + 1], ln_r[:, t:t + 1],
                                       ALU.subtract, ALU.mult))
                ins = dve.tensor_tensor(v0[:, t, :], v0[:, t, :], ln_gb[:, 0, :], ALU.mult)
                if t < TT - 1:
                    ins.then_inc(v0_normed, 1)
                else:
                    link(ins)
                    dve.tensor_tensor(v0[:, t, :], v0[:, t, :], ln_gb[:, 1, :], ALU.add).then_inc(v0_done, 1)

            def sv_add(i):
                name = f"SV{i}"
                if i >= 2:
                    dve.wait_ge(hid_done, 2 + i - 1)
                release(dve.tensor_tensor(v3(gated[:, i % 2, :], TT), v3(ready(name), TT),
                                          bsx[:, i, :].unsqueeze(1).broadcast_to([P, TT, P]), ALU.add), name)

            def gate_lo(i):
                dve.wait_ge(hid_hi_done, 2 + i + 1)
                dve.tensor_tensor(hid_lo[:, i, :], gated[:, i % 2, :], hid_hi[:, i, :].bitcast(F32),
                                  ALU.subtract).then_inc(hid_done, 1)

            for i in range(TOKT):
                if i >= 2:
                    u_scale(i)
                if i >= SPATIAL_LAG + 1:
                    gate_lo(i - SPATIAL_LAG - 1)
                if i >= SPATIAL_LAG:
                    sv_add(i - SPATIAL_LAG)
            for i in range(TOKT - SPATIAL_LAG, TOKT):
                gate_lo(i - 1)
                sv_add(i)
            gate_lo(TOKT - 1)

            def round_of(out_, in_, scale):
                link(dve.tensor_scalar(out_, in_, scale, ROUND, ALU.mult, ALU.add))
                link(dve.tensor_scalar(out_, out_, -ROUND, None, ALU.add))

            def less(a, n, c):
                link(dve.scalar_tensor_tensor(a, n, -c, a, ALU.mult, ALU.add))

            def rotation_angles(step):
                if step == 0:
                    dve.wait_ge(pos_in, 16)
                    link(dve.tensor_scalar(ang, pos_i, cols[:, C_FREQ:C_FREQ + 1], None, ALU.mult))
                    round_of(turns_n, ang, 1.0 / FAR)
                elif step == 1:
                    less(ang, turns_n, FAR_1)
                    less(ang, turns_n, FAR_2)
                    link(dve.tensor_scalar(far_t, turns_n, FAR_3, None, ALU.mult))
                elif step in (2, 4):
                    round_of(turns_n, ang, 1.0 / TWO_PI)
                elif step in (3, 5):
                    less(ang, turns_n, PI_1)
                    less(ang, turns_n, PI_2)
                    less(ang, turns_n, PI_3)
                    if step == 3:
                        link(dve.tensor_tensor(ang, ang, far_t, ALU.subtract))
                else:
                    link(dve.tensor_scalar(sin_t, ang, BELOW_PI, -BELOW_PI, ALU.min, ALU.max))
                    link(dve.scalar_tensor_tensor(far_t, sin_t, -1.0, sin_t, ALU.mult, ALU.max))
                    dve.tensor_scalar(cos_t, far_t, -1.0, np.pi / 2, ALU.mult, ALU.add).then_inc(sin_arg, 2)

            for layer in range(DEPTH):
                if layer == 1:
                    norm_factors("NS2")
                    dve.tensor_copy(scaled_mx, n_r).then_inc(n2_ready, 1)
                    cross_factors(1)
                    dve.memset(v1[0][0:CHUNK, 0, :], 0.0).then_inc(v_zeroed, 1)
                    release(dve.tensor_tensor(v3(ks_a, TT), v3(ready("KS")[:, 0:TT * KVH], TT), along(n_r2, KVH),
                                              ALU.mult), "KS")
                    dve.wait_ge(trig_done, 2)

                    def rotate_tile(tile, name, n):
                        if n - 2 >= KVH:
                            dve.wait_ge(q_rot, n - 1 - KVH)
                        release(dve.tensor_tensor(rot_s[:, n % 2, :], ready(name), sin_t, ALU.mult), name)
                        wait_read(dve, name)
                        dve.wait_ge(rot_cos, n + 1)
                        return dve.tensor_tensor(tile, tile, rot_s[:, n % 2, :], ALU.add)

                    def key_scale(g):
                        name = f"KB{g}"
                        release(dve.tensor_tensor(k1[:, g, :], k1[:, g, :], ready(name), ALU.mult), name)

                    def query_squares(g):
                        name = f"QS{g}"
                        release(dve.tensor_tensor(v3(qs_a, TT)[:, :, 4 * g:4 * g + 4], v3(ready(name)[:, 0:TT * 4], TT),
                                                  along(n_r2, 4), ALU.mult), name)

                    for g in range(KVH):
                        link(rotate_tile(k1[:, g, :], f"KR{g}", g))
                    dve.wait_ge(root_done, ROOT["ks"])
                    link(dve.reciprocal(ks_b, ks_b))
                    link(dve.tensor_tensor(v3(ks_r, TT), v3(ks_b, TT), along(n_r, KVH), ALU.mult))
                    diagonal("kb0", v3(ks_r, TT)[:, :, 0])
                    cross_step(1, 0)
                    diagonal("kb1", v3(ks_r, TT)[:, :, 1])
                    rotate_tile(q1[:, 0, :], "QR0", KVH).then_inc(q_rot, 1)
                    cross_step(1, 1)
                    for i in range(1, TOKT):
                        if i <= KVH:
                            key_scale(i - 1)
                        if i == 1:
                            diagonal("kb2", v3(ks_r, TT)[:, :, 2])
                        cross_step(1, 2 * i)
                        rotate_tile(q1[:, i, :], f"QR{i}", KVH + i).then_inc(q_rot, 1)
                        if i % 2:
                            query_squares(i // 2)
                        cross_step(1, 2 * i + 1)
                    dve.wait_ge(root_done, ROOT["qs"])
                    link(dve.reciprocal(qs_b, qs_b))
                    link(dve.scalar_tensor_tensor(v3(qs_r, TT), v3(qs_b, TT), QK_SCALE, along(n_r, HEADS),
                                                  ALU.mult, ALU.mult))

                    def swa_max(w):
                        g, j = divmod(w, TT)
                        b = w % 2
                        m = mx[:, 4 * b:4 * b + 4]
                        banks = [v3(ready(f"S{e}{w}")[:, 0:2 * P], 2) for e in "AB"]
                        if j == 0:
                            for s in banks:
                                ins = dve.memset(s[0:CHUNK, :, 0:CHUNK], NO_KEY)
                            link(ins)
                        for e, s in enumerate(banks):
                            ins = dve.tensor_reduce(m[:, 2 * e:2 * e + 2], s, AX, ALU.max)
                        link(ins)
                        link(dve.tensor_tensor(scaled_mx, m, v3(qs_r, TT)[:, j, 4 * g:4 * g + 4], ALU.mult))
                        nm = neg_m[:, 4 * b:4 * b + 4]
                        link(dve.scalar_tensor_tensor(nm, scaled_mx, -1.0, neg_sink[:, 4 * g:4 * g + 4],
                                                      ALU.mult, ALU.min))
                        dve.tensor_tensor(sink_d[:, 4 * b:4 * b + 4], nm,
                                          cols[:, C_SINK + 4 * g:C_SINK + 4 * g + 4], ALU.add).then_inc(neg_m_done, 1)

                    def swa_inverse(w):
                        b = w % 2
                        wait_read(dve, f"SB{w}")
                        dve.wait_ge(sink_exp, w + 1)
                        if w:
                            dve.wait_ge(inv_done, w)
                        link(dve.tensor_tensor(tot, sums[:, 4 * b:4 * b + 4], sink_e[:, 4 * b:4 * b + 4], ALU.add))
                        if w >= 2:
                            dve.wait_ge(pn_swa, w - 1)
                        dve.reciprocal(inv[:, 4 * b:4 * b + 4], tot).then_inc(inv_done, 1)

                    def swa_pT(w):
                        U = 2 * CROSS_UNITS + w
                        dve.wait_ge(t_done, U + 1)
                        dve.wait_ge(o_done, U - 1)
                        dve.tensor_copy(probsT[:, w % 2, :], swa_t(w)).then_inc(pT_dve, 1)

                    def swa_out(m):
                        g, jj = divmod(m, 2)
                        dve.wait_ge(hid_hi_done, HID_L + 2 + m + 1)

                        def part(a):
                            return a[:, 2 * g:2 * g + 2, 2 * jj * P:(2 * jj + 2) * P].rearrange(
                                "p i (j t) -> p j i t", j=2)
                        dve.tensor_tensor(part(hid_lo), swa_o(m).rearrange("p (j i t) -> p j i t", j=2, i=2),
                                          part(hid_hi).bitcast(F32), ALU.subtract).then_inc(hid_done, 1)

                    for w in range(SWA_UNITS + 3):
                        if w < SWA_UNITS:
                            swa_max(w)
                        if 1 <= w <= SWA_UNITS:
                            swa_inverse(w - 1)
                        if 2 <= w < SWA_UNITS + 2:
                            swa_pT(w - 2)
                        if w >= 4 and w % 2 == 0:
                            swa_out((w - 4) // 2)

                for d in range(KT):
                    out_update(layer, d)
                    if d >= 1:
                        prepare_lo(1 + 2 * layer, d - 1, C_MLP[layer])
                prepare_lo(1 + 2 * layer, KT - 1, C_MLP[layer])
                for t in range(KT):
                    tn = TURN[f"UP{layer}_0_{t}"]
                    mlp_up(layer, 0, t, bank(tn), tn // ACC + 1)
                    if t == 1:
                        norm_factors(f"NS{1 + 2 * layer}")
                        diagonal(f"n{1 + 2 * layer}", n_r2)
                    if layer == 0 and t >= 1:
                        rotation_angles(t - 1)
                wait_read(dve, f"RB{1 + 2 * layer}")
                body = TURN[f"DN{layer}_0_0"]
                with dve.Fori(0, QUARTERS - 1) as q:
                    for j in range(2 * KT):
                        n_read = q * (2 * KT // ACC) + ((body + j) // ACC + 1)
                        if j < KT:
                            mlp_down(layer, q, j, q * (2 * KT) + (body + j), bank(body + j), n_read)
                        else:
                            mlp_up(layer, q + 1, j - KT, bank(body + j), n_read)
                for t in range(KT):
                    tn = TURN[f"DN{layer}_{QUARTERS - 1}_{t}"]
                    mlp_down(layer, QUARTERS - 1, t, tn, bank(tn), tn // ACC + 1)
                    if layer < DEPTH - 1 and t >= 1:
                        prepare_lo(2 * (layer + 1), t - 1, C_MIX[layer + 1])
                if layer < DEPTH - 1:
                    prepare_lo(2 * (layer + 1), KT - 1, C_MIX[layer + 1])

        @block.tensor
        def _(pe):
            def open_turn(name):
                t = TURN[name]
                if t >= ACC:
                    pe.wait_ge(acc_free[bank(t)], t // ACC)
                return acc_of(name)

            def close(ins):
                ins.then_inc(turn_done, 1)

            def split_product(out_, st, mv, start, stop):
                pe.matmul(out_, st[0], mv[0], start=start, stop=False)
                pe.matmul(out_, st[0], mv[1], start=False, stop=False)
                return pe.matmul(out_, st[1], mv[0], start=False, stop=stop)

            def weight(h, k, n=1, width=None):
                s = slot(h, n)
                s = slice(s.start, s.start + width) if width else s
                return w_hi[:, k, s], w_lo[:, k, s]

            def both(hi, lo, k, s):
                return hi[:, k, s], lo[:, k, s]

            ALL = slice(0, SEQ)

            def project(out_, h, hi, lo, order=range(KT), before=None, start=True, stop=True, s=ALL):
                order = list(order)
                for k in order:
                    if before:
                        before(k)
                    ins = split_product(out_, weight(h, k), both(hi, lo, k, s), start and k == order[0],
                                        stop and k == order[-1])
                return ins

            def project_x(name, h, norm=None):
                out_ = open_turn(name)
                pe.wait_ge(w_ready, h + 1)
                close(project(out_, h, xg_hi, xg_lo, before=None if norm is None else
                              lambda k: pe.wait_ge(xg_lo_done, KT * norm + k + 1)))

            def project_tokens(name, h, t, width):
                out_ = open_turn(name)
                pe.wait_ge(w_ready, h + 2)
                for k in range(KT):
                    xs = both(xg_hi, xg_lo, k, slice(t * P, (t + 1) * P))
                    ins = split_product(out_[:, 0:width], xs, weight(h, k, 2, width), k == 0, k == KT - 1)
                close(ins)

            def norm_sums(n):
                out_ = open_turn(f"NS{n}")
                pe.wait_ge(sq_added, KT * (n + 1))
                for t in range(TT):
                    ins = pe.matmul(out_[:, t:t + 1], sq_sum[:, t * P:(t + 1) * P], ones[:, 0:1], start=True, stop=True)
                close(ins)

            def spread(turn_name, diag_name):
                out_ = open_turn(turn_name)
                pe.wait_ge(diag_done, DIAG[diag_name])
                close(pe.matmul(out_, ones[:], diag[:, DIAG[diag_name] % 2, :, :].rearrange("p a b -> p (a b)"),
                                start=True, stop=True))

            def cross_squares(layer):
                wait_read(pe, f"XQ{layer}_0")
                wait_read(pe, f"XQ{layer}_1")
                out_ = open_turn(f"XS{layer}")
                for i in range(2):
                    for t in range(TT):
                        c = t * XH + 2 * i
                        ins = pe.matmul(out_[:, c:c + 2], qx_sq[:, i, t * P:(t + 1) * P], blocks, start=True, stop=True)
                close(ins)

            def cross_scores(layer, u):
                U = CROSS_UNITS * layer + u
                i, th, h2 = u // 4, (u // 2) % 2, u % 2
                po = slice(h2 * HD, (h2 + 1) * HD)
                if u == 0:
                    pe.wait_ge(kmem_done, layer + 1)
                if U >= 2:
                    pe.wait_ge(exp_done, U - 1)
                for t2 in range(2):
                    t = 2 * th + t2
                    ins = pe.matmul(s_bank[:, h2, t2 * MEM:(t2 + 1) * MEM], qx[po, i, t * P:(t + 1) * P],
                                    kmem[po, layer, i, :], start=True, stop=True)
                ins.then_inc(s_done, 1)

            def cross_transpose(layer, u):
                U = CROSS_UNITS * layer + u
                pe.wait_ge(pn_cross, U + 1)
                if U:
                    pe.wait_ge(pT_act, U)
                for m in range(MT):
                    for t2 in range(2):
                        c = t2 * MEM + m * P
                        ins = pe.transpose(t_bank[:, (2 * m + t2) * P:(2 * m + t2 + 1) * P],
                                           probs[:, U % 2, c:c + P], ident)
                ins.then_inc(t_done, 1)

            def cross_values(layer, u):
                U = CROSS_UNITS * layer + u
                i, th, h2 = u // 4, (u // 2) % 2, u % 2
                h = 2 * i + h2
                pe.wait_ge(pT_act, U + 1)
                if u % 4 == 0 and U:
                    pe.wait_ge(hid_done, HID_L * layer + 1 if u else hid_after(layer - 1))
                for m in range(MT):
                    ins = pe.matmul(o_bank[h2 * HD:(h2 + 1) * HD, th * 2 * P:(th + 1) * 2 * P],
                                    vmem[:, layer, m, h * HD:(h + 1) * HD],
                                    probsT[:, U % 2, m * 2 * P:(m + 1) * 2 * P], start=(m == 0), stop=(m == MT - 1))
                ins.then_inc(o_done, 1)

            def hid_after(layer):
                return HID_L * (layer + 1)

            def cross_step(layer, s):
                if s < CROSS_UNITS:
                    cross_scores(layer, s)
                if 2 <= s < CROSS_UNITS + 2:
                    cross_transpose(layer, s - 2)
                if 3 <= s < CROSS_UNITS + 3:
                    cross_values(layer, s - 3)

            def up(layer, q, t, h, w_count, free, norm=None):
                b = bank(TURN[f"UP{layer}_{q}_{t}"])
                pe.wait_ge(acc_free[b], free)
                pe.wait_ge(w_ready, w_count)
                close(project(acc[:, b, :], h, xg_hi, xg_lo, before=None if norm is None else
                              lambda k: pe.wait_ge(xg_lo_done, KT * norm + k + 1)))

            def down(layer, t, h, w_count, b, free, hid_base):
                pe.wait_ge(acc_free[b], free)
                pe.wait_ge(w_ready, w_count)
                close(project(acc[:, b, :], h, hid_hi, hid_lo,
                              before=(lambda k: pe.wait_ge(hid_done, hid_base + (k + 1))) if t == 0 else None))

            def mem_keys(l):
                out_ = open_turn(f"MK{l}")
                for i in range(2):
                    h = H_MEMK[l] + i
                    pe.wait_ge(w_ready, h + 1)
                    ins = project(out_[:, i * MEM:(i + 1) * MEM], h, hid_hi, hid_lo, s=slice(l * MEM, (l + 1) * MEM),
                                  before=lambda k: pe.wait_ge(mem_lo, KT * l + k + 1))
                close(ins)

            for l in range(DEPTH):
                mem_keys(l)

            def mem_values(l):
                out_ = open_turn(f"MV{l}")
                h = H_MEMV[l]
                pe.wait_ge(w_ready, h + 2)
                for m in range(MT):
                    for k in range(KT):
                        s = slice(l * MEM + m * P, l * MEM + (m + 1) * P)
                        ins = split_product(out_[:, m * XW:(m + 1) * XW], both(hid_hi, hid_lo, k, s),
                                            weight(h, k, 2), k == 0, k == KT - 1)
                close(ins)

            mem_values(0)
            out_ = open_turn("MS")
            pe.wait_ge(ones_set, 1)
            pe.wait_ge(memsq_added, 1)
            for m in range(MT):
                ins = pe.matmul(out_[:, m:m + 1], mem_sq[:, 0, m * P:(m + 1) * P], ones[:, 0:1], start=True, stop=True)
            close(ins)
            pe.wait_ge(tabs_in, 16)
            pe.wait_ge(eps_set, 1)
            for l in range(DEPTH):
                out_ = open_turn(f"KN{l}")
                wait_read(pe, f"MK{l}")
                pe.matmul(out_, same_head, k_sq0[:, l, :], start=True, stop=False)
                close(pe.matmul(out_, eps_share[:], mem_sq[:, 0:1, :].broadcast_to([P, 2, MEM]), start=False, stop=True))
            mem_values(1)

            norm_sums(0)
            project_x("XQ0_0", H_XQ[0], norm=0)
            project_x("XQ0_1", H_XQ[0] + 1)
            step = 0
            for c in range(TOKT // 2):
                for t in range(TT):
                    project_tokens(f"V0_{c}_{t}", H_V0 + 2 * c, t, 2 * P)
                    if (c, t) == (0, 0):
                        cross_squares(0)
                        spread("RB0", "n0")
                    if step < CROSS_UNITS + 3:
                        cross_step(0, step)
                    step += 1

            def spatial(i):
                out_ = open_turn(f"SV{i}")
                pe.wait_ge(v0_done, TT)
                pe.wait_ge(wsT_masked, 1)
                lo, hi = i * P // GC, ((i + 1) * P - 1) // GC
                for n in range(TT):
                    for g in range(lo, hi + 1):
                        a, z = max(g * GC, i * P), min((g + 1) * GC, (i + 1) * P)
                        ins = pe.matmul(out_[a - i * P:z - i * P, n * P:(n + 1) * P], v0[:, n, a:z], wsT[:, g, :],
                                        start=True, stop=True)
                close(ins)

            for i in range(TOKT):
                project_x(f"U{i}", H_U0 + i)
                if i >= SPATIAL_LAG:
                    spatial(i - SPATIAL_LAG)
            for i in range(TOKT - SPATIAL_LAG, TOKT):
                spatial(i)

            for layer in range(DEPTH):
                if layer == 1:
                    project_x("XQ1_0", H_XQ[1], norm=2)
                    project_x("XQ1_1", H_XQ[1] + 1)
                    norm_sums(2)
                    for t in range(TT):
                        project_tokens(f"V1_{t}", H_V1, t, KVH * HD)
                        if t == 0:
                            cross_squares(1)
                    for g in range(KVH):
                        project_x(f"K{g}", H_K1 + g)
                    project_x("Q0", H_Q1)
                    out_ = open_turn("KS")
                    for g in range(KVH):
                        wait_read(pe, f"K{g}")
                        for t in range(TT):
                            ins = pe.matmul(out_[:, t * KVH + g:t * KVH + g + 1], k_sq[:, g, t * P:(t + 1) * P],
                                            blocks[:, 0:1], start=True, stop=True)
                    close(ins)

                    def rotated(name, tile, source):
                        wait_read(pe, source)
                        close(pe.matmul(open_turn(name), rotate, tile, start=True, stop=True))

                    def query_squares(g):
                        out_ = open_turn(f"QS{g}")
                        for i in range(2):
                            for t in range(TT):
                                ins = pe.matmul(v3(out_[:, 4 * t:4 * t + 4], 2)[:, :, i],
                                                qx_sq[:, i, t * P:(t + 1) * P], blocks, start=True, stop=True)
                        close(ins)

                    for g in range(KVH):
                        rotated(f"KR{g}", k1[:, g, :], f"K{g}")
                    cross_step(1, 0)
                    rotated("QR0", q1[:, 0, :], "Q0")
                    cross_step(1, 1)
                    for i in range(1, TOKT):
                        project_x(f"Q{i}", H_Q1 + i)
                        if i <= KVH:
                            spread(f"KB{i - 1}", f"kb{i - 1}")
                        cross_step(1, 2 * i)
                        rotated(f"QR{i}", q1[:, i, :], f"Q{i}")
                        if i % 2:
                            query_squares(i // 2)
                        cross_step(1, 2 * i + 1)

                    def swa_scores(w):
                        g, j = divmod(w, TT)
                        if j == 0:
                            wait_read(pe, f"KB{g}")
                            pe.wait_ge(q_rot, 2 * g + 2)
                        for e in range(2):
                            out_ = open_turn(f"S{'AB'[e]}{w}")
                            po = slice(e * HD, (e + 1) * HD)
                            for i in range(2):
                                for c in range(2):
                                    first = j * P + (c - 1) * CHUNK
                                    skip = max(0, -first)
                                    ins = pe.matmul(out_[c * CHUNK:(c + 1) * CHUNK, i * P + skip:(i + 1) * P],
                                                    q1[po, 2 * g + i, j * P + c * CHUNK:j * P + (c + 1) * CHUNK],
                                                    k1[po, g, first + skip:first + P], start=True, stop=True)
                            close(ins)

                    def swa_transpose(w):
                        pe.wait_ge(pn_swa, w + 1)
                        if w >= 2:
                            pe.wait_ge(pT_dve, w - 1)
                        else:
                            pe.wait_ge(pT_act, 2 * CROSS_UNITS)
                            pe.wait_ge(exp_done, 2 * CROSS_UNITS)
                        for e in range(4):
                            ins = pe.transpose(swa_t(w)[:, e * P:(e + 1) * P], probs[:, w % 2, e * P:(e + 1) * P], ident)
                        ins.then_inc(t_done, 1)

                    def swa_values(w):
                        g, j = divmod(w, TT)
                        m, jj = divmod(w, 2)
                        if jj == 0:
                            pe.wait_ge(hid_done, HID_L + 2 + max(0, m - 1))
                        if w == 0:
                            pe.wait_ge(v_shifted, 32)
                            pe.wait_ge(v_zeroed, 1)
                            for t in range(TT):
                                wait_read(pe, f"V1_{t}")
                        pe.wait_ge(pT_dve, w + 1)
                        o = swa_o(m).rearrange("p (j i t) -> p j i t", j=2, i=2)
                        pT = v3(probsT[:, w % 2, :], 4)
                        for c in range(2):
                            cs = slice(c * CHUNK, (c + 1) * CHUNK)
                            for e in range(2):
                                ins = pe.matmul(o[e * HD:(e + 1) * HD, jj, :, cs], v1[c][:, j, g * HD:(g + 1) * HD],
                                                pT[:, 2 * e:2 * e + 2, cs], start=True, stop=True)
                        ins.then_inc(o_done, 1)

                    for w in range(SWA_UNITS + 3):
                        if w < SWA_UNITS:
                            swa_scores(w)
                        if 2 <= w < SWA_UNITS + 2:
                            swa_transpose(w - 2)
                        if w >= 3:
                            swa_values(w - 3)

                h = H_OUT[layer]
                mixed = HID_L * layer
                if layer == 0:
                    ready_at = {6: 1, 7: 2} | {i: 3 + i for i in range(TOKT)}
                else:
                    ready_at = {6: 1, 7: 2} | {i: 4 + 2 * (i // 2) for i in range(TOKT)}

                def heads_ready(k):
                    pe.wait_ge(hid_done, mixed + ready_at[k])

                late = 2
                order = [6, 7, *range(TOKT)]
                outs = []
                for d in range(SLOTS):
                    outs.append(open_turn(f"OUT{layer}_{d}"))
                    pe.wait_ge(w_ready, h + d + 1)
                    project(outs[d], h + d, hid_hi, hid_lo, order[:-late], heads_ready if d == 0 else None, stop=False)
                for d in range(SLOTS):
                    close(project(outs[d], h + d, hid_hi, hid_lo, order[-late:], heads_ready if d == 0 else None,
                                  start=False))
                for d in range(SLOTS, KT):
                    out_ = open_turn(f"OUT{layer}_{d}")
                    pe.wait_ge(w_ready, h + d + 1)
                    close(project(out_, h + d, hid_hi, hid_lo))

                n = 1 + 2 * layer
                for t in range(KT):
                    tn = TURN[f"UP{layer}_0_{t}"]
                    up(layer, 0, t, H_MLP[layer] + t, H_MLP[layer] + t + 1, tn // ACC, n if t == 0 else None)
                    if t == 1:
                        norm_sums(n)
                    if t == 3:
                        spread(f"RB{n}", f"n{n}")
                body = TURN[f"DN{layer}_0_0"]
                hb = H_MLP[layer] + KT
                hid0 = HID_L * layer + KT
                with pe.Fori(0, QUARTERS - 1) as q:
                    for j in range(2 * KT):
                        w_count = q * (2 * KT) + (hb + j + 1)
                        free = q * (2 * KT // ACC) + ((body + j) // ACC)
                        if j < KT:
                            down(layer, j, hb + j, w_count, bank(body + j), free, q * KT + hid0)
                        else:
                            up(layer, 1, j - KT, hb + j, w_count, free)
                hb += 2 * KT * (QUARTERS - 1)
                for t in range(KT):
                    tn = TURN[f"DN{layer}_{QUARTERS - 1}_{t}"]
                    down(layer, t, hb + t, hb + t + 1, bank(tn), tn // ACC, hid0 + (QUARTERS - 1) * KT)


def tiled(a):
    return a.reshape(-1, P, a.shape[-1]).transpose(1, 0, 2)


def weight_halves(w):
    return tiled(w).reshape(P, KT, -1, P).transpose(2, 0, 1, 3).reshape(-1, P, KT * P)


def lay_out(a):
    f = np.float32
    w = []

    def add(m):
        w.append(weight_halves(m))

    for l in range(DEPTH):
        add(a["w_mem_kv"][l][:, :XW])
    for l in range(DEPTH):
        add(a["w_mem_kv"][l][:, XW:])
    ain, bin_ = a["a_w_in"][0], a["b_w_in"][0]
    kv = KVH * HD
    for l, w_out in ((0, a["a_w_out"][0]), (1, a["b_w_out"][0])):
        if l == 0:
            add(ain[:, 2 * TOK:])
            add(ain[:, TOK:2 * TOK])
            add(ain[:, :TOK])
        else:
            add(bin_[:, TOK + 2 * kv:])
            add(np.concatenate([bin_[:, TOK + kv:TOK + 2 * kv], np.zeros((D, 2 * P - kv), f)], 1))
            for g in range(KVH):
                k = bin_[:, TOK + g * HD:TOK + (g + 1) * HD]
                add(np.concatenate([k, k], 1))
            add(bin_[:, :TOK])
        add(w_out)
        for q in range(QUARTERS):
            add(a["w_up"][l][:, q * D:(q + 1) * D])
            add(a["w_down"][l][q * D:(q + 1) * D])
    halves = np.concatenate(w, 0)
    halves = np.concatenate([halves, np.zeros((2 * PAIRS - HALVES, P, KT * P), f)], 0)
    weights = halves.reshape(PAIRS, 2, P, KT * P).transpose(0, 2, 1, 3).reshape(PAIRS, P, 2 * KT * P)

    cols = np.zeros((P, N_COLS), f)
    for l in range(DEPTH):
        for at, name in ((C_MIX, "ln_mix"), (C_MLP, "ln_mlp"), (C_MEM, "ln_mem")):
            cols[:, at[l]:at[l] + KT] = a[name][l].reshape(KT, P).T
        cols[:, C_XQ[l]] = np.tile(a["xq_norm"][l], 2)
        cols[:, C_XK[l]] = np.tile(a["xk_norm"][l], 2)
    cols[:, C_BQ] = np.tile(a["b_q_norm"][0], 2)
    cols[:, C_BK] = np.tile(a["b_k_norm"][0], 2)
    half = ROPE_DIM // 2
    freq = np.power(f(ROPE_THETA), -np.arange(0, ROPE_DIM, 2, dtype=f) / f(ROPE_DIM))
    for p in range(P):
        if p % HD < ROPE_DIM:
            cols[p, C_FREQ] = freq[p % HD % half]
    cols[:, C_EPS] = EPS
    cols[:, C_EPS_SQ] = EPS * EPS
    cols[:, C_SINK:] = a["b_sinks"][0].reshape(KVH, 2, 2).transpose(0, 2, 1).reshape(1, HEADS)

    tabs = np.zeros((P, 3, P), f)
    tabs[:, 0] = np.eye(P, dtype=f)
    for p in range(P):
        if p % HD < half:
            tabs[p + half, 1, p] = -1.0
            tabs[p, 1, p + half] = 1.0
        tabs[p, 2, p // HD * HD:(p // HD + 1) * HD] = 1.0
    channel_group = np.arange(TOK) // GC
    bsx = a["a_b_s"][0][channel_group].reshape(TOKT, P, P).transpose(1, 0, 2)
    return {
        "xT": tiled(a["x"][0].T), "memT": tiled(a["mem"][0].T), "pos": a["positions"][0], "W": weights,
        "cols_d": cols, "tabs_d": tabs, "ln_d": np.stack([a["a_ln_g"][0], a["a_ln_b"][0]]), "bsx_d": bsx,
        "wsT_d": a["a_w_s"][0].transpose(2, 0, 1),
    }


def kernel(**inputs):
    import concourse.bacc as bacc
    from concourse.bass_utils import run_bass_kernel_spmd

    laid = lay_out({k: np.asarray(v) for k, v in inputs.items()})
    nc = bacc.Bacc("TRN2", target_bir_lowering=False, num_devices=1)
    arrays, args = {}, {}
    for name, a in laid.items():
        a = np.ascontiguousarray(a)
        arrays[f"in_{name}"] = a
        args[name] = nc.dram_tensor(f"in_{name}", a.shape, mybir.dt.from_np(a.dtype), kind="ExternalInput").ap()
    args["out"] = nc.dram_tensor("out_T", (P, KT, SEQ), F32, kind="ExternalOutput").ap()
    build(nc, **args)
    r = run_bass_kernel_spmd(nc, [arrays], core_ids=[0])
    o = r.results[0]["out_T"]
    return o.transpose(1, 0, 2).reshape(D, SEQ).T[None]
```

```python
from contextlib import ExitStack

import numpy as np

import concourse.bass as bass
from concourse import mybir

F32 = mybir.dt.float32
F32R = mybir.dt.float32r
I32 = mybir.dt.int32
ALU = mybir.AluOpType
ACT = mybir.ActivationFunctionType
AX = mybir.AxisListType.X

P = 128
D = 1024
SEQ = 512
DEPTH = 2
MEM = 256
HD = 64
XH = 4
XW = XH * HD
TOK = D - XW
GROUPS = 4
GC = TOK // GROUPS
HEADS = TOK // HD
KVH = 3
CHUNK = 64
DFF = 4 * D
ROPE_DIM = HD // 4
ROPE_THETA = 500000.0
EPS = 1e-6
QK_SCALE = HD ** -0.5

KT = D // P
TT = SEQ // P
MT = MEM // P
TOKT = TOK // P
QUARTERS = DFF // D
SLOTS = 4
SWA_UNITS = KVH * TT
CROSS_UNITS = 2 * XH
WARM_UP = 10
SPATIAL_LAG = 3

H_MEMK = [0, 2]
H_MEMV = [4, 6]
H_L0 = 8
H_XQ = [H_L0, H_L0 + 2 + 2 * TOKT + KT + 2 * QUARTERS * KT]
H_V0 = H_XQ[0] + 2
H_U0 = H_V0 + TOKT
H_OUT0 = H_U0 + TOKT
H_MLP0 = H_OUT0 + KT
H_V1 = H_XQ[1] + 2
H_KQ = H_V1 + 2
H_OUT1 = H_KQ + KVH // 2 + 1 + TOKT
H_MLP1 = H_OUT1 + KT
H_OUT = [H_OUT0, H_OUT1]
H_MLP = [H_MLP0, H_MLP1]
HALVES = H_MLP1 + 2 * QUARTERS * KT
PAIRS = (HALVES + 1) // 2
assert H_XQ[1] == H_MLP0 + 2 * QUARTERS * KT and HALVES == 178
assert H_V1 % SLOTS <= SLOTS - 2 and all(h % 2 == 0 for h in (*H_MEMV, H_V0))


KQ = [("K", 0), ("Q", 0), ("Q", 1), ("K", 1)] + [("Q", i) for i in range(2, TOKT)]
SWA_STEPS = SWA_UNITS + 3
CROSS_STEPS = CROSS_UNITS + 3
STEPS_KQ = [
    ([("C", 1)], [("C", 2)]),
    ([("C", 3)], [("C", 4)]),
    ([("C", 5)], [("C", 6)]),
    ([("C", 7), ("QN", 0), ("KN", 0)], [("C", 8), ("KR", 0), ("KS", 0)]),
    ([("C", 9), ("KC", 0)], [("C", 10)]),
    ([("S", 0)], [("S", 1)]),
    ([("QN", 1)], [("KN", 1), ("S", 2)]),
    ([("KR", 1), ("KS", 1)], [("S", 3), ("S", 4), ("QN", 2), ("S", 5)] + [("S", w) for w in range(6, SWA_UNITS)]),
]
assert TT == 4 and KVH == 3 and CROSS_STEPS == 11 and len(STEPS_KQ) == len(KQ)


def plan_turns():
    order, used = [], {}

    def turn(name, *halves):
        for h in halves:
            used[h] = len(order)
        order.append(name)

    turn("MK0", 0, 1)
    turn("MK1", 2, 3)
    turn("MS")
    turn("MV0", 4, 5)
    turn("KN0")
    turn("KN1")
    turn("MV1", 6, 7)
    turn("XQ0_0", H_XQ[0])
    turn("XQ0_1", H_XQ[0] + 1)
    turn("NS0")
    for c in range(TOKT // 2):
        for t in range(TT):
            turn(f"V0_{c}_{t}", *((H_V0 + 2 * c, H_V0 + 2 * c + 1) if t == TT - 1 else ()))
            if (c, t) == (0, 0):
                turn("XS0")
                turn("RB0")
    for i in range(TOKT):
        turn(f"U{i}", H_U0 + i)
        if i >= SPATIAL_LAG:
            turn(f"SV{i - SPATIAL_LAG}")
    for i in range(TOKT - SPATIAL_LAG, TOKT):
        turn(f"SV{i}")
    for layer in range(DEPTH):
        if layer == 1:
            turn("XQ1_0", H_XQ[1])
            turn("XQ1_1", H_XQ[1] + 1)
            turn("NS2")
            for t in range(TT):
                turn(f"V1_{t}", *((H_V1, H_V1 + 1) if t == TT - 1 else ()))
                if t == 0:
                    turn("XS1")
            for n, (kind, i) in enumerate(KQ):
                for part, todo in enumerate(STEPS_KQ[n]):
                    if part == 1:
                        turn(f"{kind}{i}", H_KQ + n)
                    for step, j in todo:
                        if step in ("KN", "QN"):
                            turn(f"{step}{j}_1")
                        elif step == "S":
                            turn(f"SA{j}")
                            turn(f"SB{j}")
        for d in range(KT):
            turn(f"OUT{layer}_{d}", H_OUT[layer] + d)
        h = H_MLP[layer]
        for t in range(KT):
            turn(f"UP{layer}_0_{t}", h + t)
            if t == 1:
                turn(f"NS{1 + 2 * layer}")
        h += KT
        for q in range(QUARTERS):
            for t in range(KT):
                turn(f"DN{layer}_{q}_{t}", h)
                h += 1
            if q < QUARTERS - 1:
                for t in range(KT):
                    turn(f"UP{layer}_{q + 1}_{t}", h)
                    h += 1
    return {n: i for i, n in enumerate(order)}, used


TURN, USED_UP = plan_turns()
ACC = 4

C_MIX = [0, 8]
C_MLP = [16, 24]
C_MEM = [32, 40]
C_XQ = [48, 49]
C_XK = [50, 51]
C_BQ, C_BK = 52, 53
C_FREQ, C_EPS, C_EPS_SQ = 54, 55, 56
C_SINK = 57
N_COLS = C_SINK + HEADS


def high_bits(x, bits):
    e = np.floor(np.log2(abs(x))) + 1 - bits
    return float(np.floor(x / 2.0 ** e) * 2.0 ** e)


TWO_PI = 2 * np.pi
ROUND = float(1.5 * 2 ** 23)
FAR = TWO_PI * 2 ** 13
FAR_1 = high_bits(FAR, 8)
FAR_2 = high_bits(FAR - FAR_1, 8)
FAR_3 = float(FAR - FAR_1 - FAR_2)
PI_1 = high_bits(TWO_PI, 11)
PI_2 = high_bits(TWO_PI - PI_1, 11)
PI_3 = float(TWO_PI - PI_1 - PI_2)
BELOW_PI = 3.1415925
NO_KEY = -1e30


def build(nc, xT, memT, pos, W, cols_d, tabs_d, ln_d, bsx_d, wsT_d, out):
    with ExitStack() as ctx:
        def sb(name, shape, dt=F32):
            return ctx.enter_context(nc.sbuf_tensor(name, shape, dt))

        def psum(name, shape):
            return ctx.enter_context(nc.psum_tensor(name, shape, F32))

        def sem(name):
            return ctx.enter_context(nc.semaphore(name))

        x = sb("x", [P, KT, SEQ])
        xg_hi = sb("xg_hi", [P, KT, SEQ], F32R)
        xg_lo = sb("xg_lo", [P, KT, SEQ], F32R)
        hid_hi = sb("hid_hi", [P, KT, SEQ], F32R)
        hid_lo = sb("hid_lo", [P, KT, SEQ], F32R)
        w_raw = sb("w_raw", [P, SLOTS, KT * P])
        w_hi = sb("w_hi", [P, KT, SLOTS * P], F32R)
        w_lo = sb("w_lo", [P, KT, SLOTS * P], F32R)
        cols = sb("cols", [P, N_COLS])
        tabs = sb("tabs", [P, 2, P])
        ident, same_head = tabs[:, 0, :], tabs[:, 1, :]
        blocks = same_head.rearrange("p (h n) -> p h n", h=2)[:, :, 0]
        ones = sb("ones", [P, P])
        eps_share = sb("eps_share", [P, P])
        kmem = sb("kmem", [P, DEPTH, 2, MEM])
        vmem = sb("vmem", [P, DEPTH, MT, XW])
        diag = sb("diag", [P, 4, P])
        x_sq = sb("x_sq", [P, 2, SEQ])
        sq_sum = sb("sq_sum", [P, SEQ])
        r_row = sb("r_row", [P, SEQ])
        small = sb("small", [P, 512])
        probs = sb("probs", [P, 2, 512])
        probsT = sb("probsT", [P, 2, 512])
        relu, hid_sq, scaled = probs, probsT[:, 0, :], probsT[:, 1, :]
        qx = sb("qx", [P, 2, SEQ])
        qx_sq = sb("qx_sq", [P, 2, SEQ])
        gated = qx_sq
        work = sb("work", [P, 9728])

        at = [0]

        def carve(n, begin=None):
            if begin is not None:
                at[0] = begin
            at[0] += n
            return work[:, at[0] - n:at[0]]

        mem_in = carve(KT * MEM, 0).rearrange("p (k m) -> p k m", k=KT)
        mem_sq = carve(KT * MEM).rearrange("p (k m) -> p k m", k=KT)
        k_sq0 = carve(DEPTH * 2 * MEM).rearrange("p (l n) -> p l n", l=DEPTH)
        v0 = carve(TT * TOK, 0).rearrange("p (t c) -> p t c", t=TT)
        u0 = carve(TOKT * SEQ).rearrange("p (i t) -> p i t", i=TOKT)
        ln_gb = carve(2 * TOK).rearrange("p (s c) -> p s c", s=2)
        bsx = carve(TOKT * P).rearrange("p (i t) -> p i t", i=TOKT)
        wsT = carve(GROUPS * P).rearrange("p (g t) -> p g t", g=GROUPS)
        cos_t = carve(SEQ, 0)
        sin_t = carve(SEQ)
        q1 = carve(TOKT * SEQ).rearrange("p (i t) -> p i t", i=TOKT)
        k1 = carve(KVH * SEQ).rearrange("p (i t) -> p i t", i=KVH)
        v1 = [carve(TT * KVH * HD).rearrange("p (t c) -> p t c", t=TT) for _ in range(2)]
        rot_s = carve(2 * SEQ).rearrange("p (b t) -> p b t", b=2)
        swapped = [rot_s[:, 0, :], rot_s[:, 1, :], x_sq[:, 0, :], x_sq[:, 1, :]]
        k_sq = carve(2 * SEQ).rearrange("p (b t) -> p b t", b=2)
        k_first = carve(SEQ)
        key_tiles = [k_first, k1[:, 2, :]]
        ang, turns_n, far_t, pos_f = (q1[:, i, :] for i in range(4))
        pos_i = pos_f.bitcast(I32)
        kq_tiles = [key_tiles[i] if kind == "K" else q1[:, i, :] for kind, i in KQ]

        sat = [0]

        def cols_of(n):
            sat[0] += n
            return small[:, sat[0] - n:sat[0]]

        mem_r = cols_of(MT)
        mem_ms = cols_of(MT)
        n_root = cols_of(TT)
        n_r = cols_of(TT)
        n_r2 = cols_of(TT)
        xs_a = cols_of(TT * XH)
        xs_b = cols_of(TT * XH)
        xs_r = cols_of(TT * XH)
        mx = cols_of(8)
        scaled_mx = cols_of(4)
        neg_m = cols_of(8)
        sums = cols_of(8)
        sink_e = cols_of(8)
        sink_d = cols_of(8)
        inv = cols_of(8)
        tot = cols_of(4)
        ln_st = cols_of(TT * 12)
        ln_mv = cols_of(TT * 2)
        ln_r = cols_of(TT)
        ln_root = cols_of(TT)
        qs_a = cols_of(TT * HEADS)
        qs_b = cols_of(TT * HEADS)
        qs_r = cols_of(TT * HEADS)
        neg_sink = cols_of(HEADS)

        def v3(ap, a):
            return ap.rearrange("p (a b) -> p a b", a=a)

        acc = psum("acc", [P, ACC, 512])
        s_bank = psum("s_bank", [P, 2, 512])
        t_bank = psum("t_bank", [P, 512])
        o_bank = psum("o_bank", [P, 512])

        def swa_t(w):
            return s_bank[:, 0, :] if w % 2 else t_bank[:]

        def swa_o(m):
            return s_bank[:, 1, :] if m % 2 else o_bank[:]

        cols_in, tabs_in, ln_in, pos_in, v_shifted, stored = (
            sem(n) for n in ("cols_in", "tabs_in", "ln_in", "pos_in", "v_shifted", "stored"))
        mem_loaded = [sem(f"mem_loaded{i}") for i in range(4)]
        x_loaded = [sem(f"x_loaded{i}") for i in range(4)]
        part_loaded, part_hi, part_lo = sem("part_loaded"), sem("part_hi"), sem("part_lo")
        first_loaded = [sem(f"first_loaded{i}") for i in range(SLOTS)]
        w_loaded = [sem(f"w_loaded{i}") for i in range(2)]
        w_hi_done, w_ready = sem("w_hi_done"), sem("w_ready")
        ones_set, eps_set, wsT_masked, v_zeroed = sem("ones_set"), sem("eps_set"), sem("wsT_masked"), sem("v_zeroed")
        turn_done = sem("turn_done")
        acc_free = [sem(f"acc_free{i}") for i in range(ACC)]
        mem_hi, mem_lo, memsq_done, memsq_added, kmem_done = (
            sem(n) for n in ("mem_hi", "mem_lo", "memsq_done", "memsq_added", "kmem_done"))
        xg_hi_done, xg_lo_done, x_squared, sq_added = (
            sem(n) for n in ("xg_hi_done", "xg_lo_done", "x_squared", "sq_added"))
        root_done = sem("root_done")
        mem_r_ready, n2_ready = sem("mem_r_ready"), sem("n2_ready")
        diag_done = sem("diag_done")
        s_done, t_done, o_done = sem("s_done"), sem("t_done"), sem("o_done")
        neg_m_done, exp_done, sink_exp = sem("neg_m_done"), sem("exp_done"), sem("sink_exp")
        inv_done, pn_cross, pn_swa = sem("inv_done"), sem("pn_cross"), sem("pn_swa")
        pT_act, pT_dve = sem("pT_act"), sem("pT_dve")
        hid_hi_done, hid_done = sem("hid_hi_done"), sem("hid_done")
        v0_gelu, ln_stats, v0_normed, v0_done = (sem(n) for n in ("v0_gelu", "ln_stats", "v0_normed", "v0_done"))
        u_done, gated_done = sem("u_done"), sem("gated_done")
        sin_arg, trig_done = sem("sin_arg"), sem("trig_done")
        swap_zeroed, rot_cos, rotated = sem("swap_zeroed"), sem("rot_cos"), sem("rotated")
        keys_scaled, keys_copied = sem("keys_scaled"), sem("keys_copied")
        swap_in = [sem(f"swap_in{i}") for i in range(4)]
        hid_squared, x_updated = sem("hid_squared"), sem("x_updated")
        dve_step = sem("dve_step")

        block = ctx.enter_context(nc.Block())

        HID_L = KT + QUARTERS * KT
        X_L = QUARTERS * KT
        ROOT = {n: i + 1 for i, n in enumerate(["xs0", "ln", "xs1", "qs0", "qs1", "qs2"])}

        def group(ap, g):
            return v3(ap, TT)[:, :, 4 * g:4 * g + 4]

        def bank(t):
            return t % ACC

        def acc_of(name):
            return acc[:, bank(TURN[name]), :]

        def release(ins, name):
            ins.then_inc(acc_free[bank(TURN[name])], 1)

        def wait_read(eng, name):
            eng.wait_ge(acc_free[bank(TURN[name])], TURN[name] // ACC + 1)

        def slot(h, n=1):
            s = h % SLOTS
            return slice(s * P, (s + n) * P)

        @block.sync
        def _(sp):
            def load(pair, free, sems):
                sp.wait_ge(w_ready, free)
                sp.dma_start(w_raw[:, 2 * sems:2 * sems + 2, :].rearrange("p s n -> p (s n)"),
                             W[bass.ds(pair, 1), :, :].rearrange("o p n -> p (o n)")
                             if not isinstance(pair, int) else W[pair, :, :]).then_inc(w_loaded[sems], 16)

            def first(h):
                sp.dma_start(w_raw[:, h, :], W[h // 2, :, (h % 2) * KT * P:(h % 2 + 1) * KT * P]).then_inc(
                    first_loaded[h], 16)

            def load_mem(i):
                sp.dma_start(mem_in[:, 2 * i:2 * i + 2, :], memT[:, 2 * i:2 * i + 2, :]).then_inc(mem_loaded[i], 16)

            n = KT * P // 2
            sp.dma_start(w_raw[:, 0, 0:n], W[0, :, 0:n]).then_inc(part_loaded, 16)
            sp.dma_start(cols[:], cols_d).then_inc(cols_in, 16)
            load_mem(0)
            sp.dma_start(w_raw[:, 0, n:2 * n], W[0, :, n:2 * n]).then_inc(first_loaded[0], 16)
            load_mem(1)
            first(1)
            for i in range(2, 4):
                load_mem(i)
            first(2)
            first(3)
            load(2, 2, 0)
            for i in range(4):
                if i == 2:
                    load(3, 4, 1)
                sp.dma_start(x[:, 2 * i:2 * i + 2, :], xT[:, 2 * i:2 * i + 2, :]).then_inc(x_loaded[i], 16)

            def stream(begin, end):
                with sp.Fori(begin // 2, end // 2) as i:
                    for s in range(2):
                        load(2 * i + s, 4 * i + (2 * s - 2), s)

            def swap(n):
                tile = kq_tiles[n]
                wait_read(sp, "%s%d" % KQ[n])
                if n >= 4:
                    sp.wait_ge(rotated, n - 3)
                elif n == 0:
                    sp.wait_ge(swap_zeroed, 4)
                half = ROPE_DIM // 2
                for head in (0, HD):
                    for a, b in ((0, half), (half, 0)):
                        sp.dma_start(swapped[n % 4][head + a:head + a + half, :],
                                     tile[head + b:head + b + half, :]).then_inc(swap_in[n % 4], 16)

            first_pair = (H_KQ + 6) // 2
            last_pair = first_pair + (len(KQ) + 3) // 4 * 2
            assert first_pair % 2 == last_pair % 2 == 0 and PAIRS % 2 == 1
            stream(4, first_pair)
            for pair in range(first_pair, last_pair):
                load(pair, 2 * pair - 2, pair % 2)
                for h in (2 * pair - 6, 2 * pair - 5):
                    if h < H_KQ + len(KQ):
                        swap(h - H_KQ)
            stream(last_pair, PAIRS - 1)
            load(PAIRS - 1, 2 * (PAIRS - 1) - 2, 0)
            for k in range(KT):
                sp.wait_ge(x_updated, DEPTH * X_L - KT + k + 1)
                sp.dma_start(out[:, k, :], x[:, k, :]).then_inc(stored, 16)
            sp.wait_ge(stored, 16 * KT)

        @block.gpsimd
        def _(pool):
            pool.memset(ones[:], 1.0).then_inc(ones_set, 1)
            pool.memset(eps_share[:], EPS * HD / D).then_inc(eps_set, 1)

            def split(h, done):
                pool.wait_ge(w_hi_done, done)
                o = w_lo[:, :, slot(h)]
                pool.tensor_tensor(o, w_raw[:, h % SLOTS, :].rearrange("p (k n) -> p k n", k=KT),
                                   w_hi[:, :, slot(h)].bitcast(F32), ALU.subtract).then_inc(w_ready, 1)

            def splits(a, b):
                for h in range(a, b):
                    split(h, h + 1)

            def add_square(n, k):
                c = KT * n + k
                pool.wait_ge(x_squared, c + 1)
                if k == 0:
                    pool.wait_ge(turn_done, TURN[f"NS{n - 1}"] + 1)
                    if n == 3:
                        pool.wait_ge(turn_done, TURN["KN1_1"] + 1)
                    pool.tensor_copy(sq_sum[:], x_sq[:, 0, :]).then_inc(sq_added, 1)
                else:
                    pool.wait_ge(sq_added, c)
                    pool.tensor_tensor(sq_sum[:], sq_sum[:], x_sq[:, k % 2, :], ALU.add).then_inc(sq_added, 1)

            def mlp(layer):
                h0 = H_MLP[layer]
                ahead = SLOTS
                splits(h0 + ahead, h0 + KT + ahead)
                body = h0 + KT + ahead
                with pool.Fori(0, QUARTERS - 1) as q:
                    for j in range(2 * KT):
                        split(body + j, q * (2 * KT) + (body + j + 1))

            def mlp_end(layer):
                body = H_MLP[layer] + KT + SLOTS + 2 * KT * (QUARTERS - 1)
                for t in range(KT):
                    if body + t < HALVES:
                        split(body + t, body + t + 1)
                    if layer < DEPTH - 1 and t >= 1:
                        add_square(2 * (layer + 1), t - 1)
                if layer < DEPTH - 1:
                    add_square(2 * (layer + 1), KT - 1)

            pool.wait_ge(w_ready, 1)
            splits(1, 5)
            pool.wait_ge(w_ready, 6)
            splits(6, H_U0 + SLOTS + 1)
            for t in range(TT - 1):
                pool.wait_ge(v0_normed, t + 1)
                pool.tensor_tensor(v0[:, t, :], v0[:, t, :], ln_gb[:, 1, :], ALU.add).then_inc(v0_done, 1)

            def gate(i):
                wait_read(pool, f"SV{i}")
                pool.wait_ge(u_done, i + 1)
                pool.tensor_tensor(gated[:, i % 2, :], gated[:, i % 2, :], u0[:, i, :],
                                   ALU.mult).then_inc(gated_done, 1)

            for i in range(1, TOKT):
                split(H_U0 + SLOTS + i, H_U0 + SLOTS + i + 1)
                if i >= SPATIAL_LAG:
                    gate(i - SPATIAL_LAG)
            for i in range(TOKT - SPATIAL_LAG, TOKT):
                gate(i)
            for layer in range(DEPTH):
                if layer == 1:
                    def cos_part(tile, n):
                        pool.wait_ge(swap_in[n % 4], 64 * (n // 4 + 1))
                        pool.tensor_tensor(tile, tile, cos_t, ALU.mult).then_inc(rot_cos, 1)

                    def swa_normalise(w):
                        pool.wait_ge(inv_done, w + 1)
                        pool.tensor_tensor(v3(probs[:, w % 2, :], 4), v3(probs[:, w % 2, :], 4),
                                           inv[:, 4 * (w % 2):4 * (w % 2) + 4].unsqueeze(2).broadcast_to([P, 4, P]),
                                           ALU.mult).then_inc(pn_swa, 1)

                    splits(H_XQ[1] + SLOTS, H_KQ + SLOTS)
                    pool.wait_ge(trig_done, 2)
                    for n in range(len(KQ)):
                        if n:
                            cos_part(kq_tiles[n - 1], n - 1)
                        for part, todo in enumerate(STEPS_KQ[n]):
                            for step, j in todo:
                                if step == "S" and j >= 1:
                                    swa_normalise(j - 1)
                                if (step, j) == ("S", 5):
                                    cos_part(kq_tiles[-1], len(KQ) - 1)
                                if n == len(KQ) - 1 and (step, j) == ("S", 7):
                                    split(H_OUT1 + SLOTS - 1, H_OUT1 + SLOTS)
                        if n < len(KQ) - 1:
                            split(H_KQ + SLOTS + n, H_KQ + SLOTS + n + 1)
                    swa_normalise(SWA_UNITS - 1)
                for d in range(KT):
                    split(H_OUT[layer] + SLOTS + d, H_OUT[layer] + SLOTS + d + 1)
                    if d >= 1:
                        add_square(1 + 2 * layer, d - 1)
                add_square(1 + 2 * layer, KT - 1)
                mlp(layer)
                mlp_end(layer)

        @block.scalar
        def _(act):
            eps = cols[:, C_EPS:C_EPS + 1]

            def split_hi(h, loaded, s):
                if isinstance(h, int) and h < SLOTS:
                    act.wait_ge(first_loaded[h], 16)
                else:
                    act.wait_ge(w_loaded[s // 2], loaded)
                act.activation(w_hi[:, :, slot(h)], w_raw[:, s, :].rearrange("p (k n) -> p k n", k=KT),
                               ACT.Copy).then_inc(w_hi_done, 1)

            nexth = [0]

            def weights(after=None, end=HALVES):
                while nexth[0] < end:
                    h = nexth[0]
                    if h >= SLOTS:
                        if after is None or USED_UP[h - SLOTS] > TURN[after]:
                            return
                        act.wait_ge(turn_done, USED_UP[h - SLOTS] + 1)
                    split_hi(h, 16 * (h // SLOTS), h % SLOTS)
                    nexth[0] += 1

            def ready(name):
                act.wait_ge(turn_done, TURN[name] + 1)
                return acc_of(name)

            def root(out_, in_):
                act.activation(out_, in_, ACT.Sqrt, bias=eps, scale=1.0 / HD).then_inc(root_done, 1)

            def root_of_turn(name, out_, n):
                release(act.activation(out_, ready(name)[:, 0:n], ACT.Sqrt, bias=eps, scale=1.0 / D), name)

            def x_square(n, k):
                if KT * n + k >= 2:
                    act.wait_ge(sq_added, KT * n + k - 1)
                act.activation(x_sq[:, k % 2, :], x[:, k, :], ACT.Square).then_inc(x_squared, 1)

            def prepare_hi(n, k, gain, square=True):
                act.activation(xg_hi[:, k, :], x[:, k, :], ACT.Identity,
                               scale=cols[:, gain + k:gain + k + 1]).then_inc(xg_hi_done, 1)
                if square:
                    x_square(n, k)

            def q_evacuate(name, dst, gain, sq):
                src = ready(name)
                act.activation(dst, src, ACT.Identity, scale=cols[:, gain:gain + 1])
                release(act.activation(sq, src, ACT.Square), name)

            def cross_exp(layer, u):
                U = CROSS_UNITS * layer + u
                i, th, h2 = u // 4, (u // 2) % 2, u % 2
                b = U % 2
                act.wait_ge(neg_m_done, U + 1)
                if U >= 2:
                    act.wait_ge(t_done, U - 1)
                for t2 in range(2):
                    t = 2 * th + t2
                    ins = act.activation(probs[:, b, t2 * MEM:(t2 + 1) * MEM], s_bank[:, h2, t2 * MEM:(t2 + 1) * MEM],
                                         ACT.Exp, bias=neg_m[:, 4 * b + t2:4 * b + t2 + 1],
                                         scale=xs_r[:, t * XH + 2 * i + h2:t * XH + 2 * i + h2 + 1],
                                         accum_out=sums[:, 4 * b + t2:4 * b + t2 + 1])
                ins.then_inc(exp_done, 1)

            def cross_pT(layer, u):
                U = CROSS_UNITS * layer + u
                act.wait_ge(t_done, U + 1)
                if U >= 2:
                    act.wait_ge(o_done, U - 1)
                act.activation(probsT[:, U % 2, :], t_bank[:], ACT.Copy).then_inc(pT_act, 1)

            def cross_out(layer, i):
                act.wait_ge(o_done, CROSS_UNITS * layer + 4 * i + 4)
                if layer == 0:
                    act.wait_ge(turn_done, TURN["MV1"] + 1)
                act.activation(hid_hi[:, TOKT + i, :], o_bank[:], ACT.Copy).then_inc(hid_hi_done, 1)

            def cross_step(layer, s):
                if s < CROSS_UNITS:
                    cross_exp(layer, s)
                if 2 <= s < CROSS_UNITS + 2:
                    cross_pT(layer, s - 2)
                if s == 6 or s == 10:
                    cross_out(layer, (s - 6) // 4)

            def mlp_up(layer, q, t, tn, b, n_read):
                act.wait_ge(turn_done, tn + 1)
                act.wait_ge(hid_done, (q * KT) + (HID_L * layer + KT + t - 1))
                act.activation(relu[:, t % 2, :], acc[:, b, :], ACT.Relu).then_inc(acc_free[b], 1)
                act.wait_ge(acc_free[b], n_read)
                act.activation(hid_hi[:, t, :], relu[:, t % 2, :], ACT.Square).then_inc(hid_hi_done, 1)

            def first_hi(part, loaded, done):
                ks = slice(part * KT // 2, (part + 1) * KT // 2)
                act.wait_ge(loaded, 16)
                act.activation(w_hi[:, ks, slot(0)], w_raw[:, 0, :].rearrange("p (k n) -> p k n", k=KT)[:, ks, :],
                               ACT.Copy).then_inc(done, 1)

            first_hi(0, part_loaded, part_hi)
            act.wait_ge(cols_in, 16)
            for k in range(KT):
                act.wait_ge(mem_loaded[k // 2], 16)
                act.activation(hid_hi[:, k, 0:MEM], mem_in[:, k, :], ACT.Identity,
                               scale=cols[:, C_MEM[0] + k:C_MEM[0] + k + 1]).then_inc(mem_hi, 1)
                if k == 1:
                    first_hi(1, first_loaded[0], w_hi_done)
                    nexth[0] = 1
                if k == 3:
                    weights(None, 2)
            weights()
            act.dma_start(tabs[:], tabs_d).then_inc(tabs_in, 16)
            for i in range(4):
                act.activation(mem_sq[:, 2 * i:2 * i + 2, :], mem_in[:, 2 * i:2 * i + 2, :],
                               ACT.Square).then_inc(memsq_done, 1)
            def x_hi(k):
                if k % 2 == 0:
                    act.wait_ge(x_loaded[k // 2], 16)
                prepare_hi(0, k, C_MIX[0], square=False)

            for l in range(DEPTH):
                src = ready(f"MK{l}")
                act.activation(kmem[:, l, :, :], v3(src, 2), ACT.Identity,
                               scale=cols[:, C_XK[l]:C_XK[l] + 1])
                release(act.activation(k_sq0[:, l, :], src, ACT.Square), f"MK{l}")
                if l == 1:
                    root_of_turn("MS", mem_ms, MT)
                weights(f"MK{l}")
                for k in range(l * KT // 2, (l + 1) * KT // 2):
                    x_hi(k)
            act.dma_start(ln_gb, ln_d.unsqueeze(0).broadcast_to([P, 2, TOK])).then_inc(ln_in, 16)
            act.dma_start(bsx, bsx_d).then_inc(ln_in, 16)
            act.dma_start(wsT, wsT_d).then_inc(ln_in, 16)

            def mem_values(l):
                src = ready(f"MV{l}")
                act.wait_ge(mem_r_ready, 1)
                for m in range(MT):
                    ins = act.activation(vmem[:, l, m, :], src[:, m * XW:(m + 1) * XW], ACT.Identity,
                                         scale=mem_r[:, m:m + 1])
                release(ins, f"MV{l}")
                weights(f"MV{l}")

            mem_values(0)
            for l in range(DEPTH):
                name = f"KN{l}"
                release(act.activation(k_sq0[:, l, :], ready(name), ACT.Sqrt, bias=cols[:, C_EPS_SQ:C_EPS_SQ + 1],
                                       scale=1.0 / HD), name)
            for k in range(KT):
                x_square(0, k)
            mem_values(1)

            for i in range(2):
                q_evacuate(f"XQ0_{i}", qx[:, i, :], C_XQ[0], qx_sq[:, i, :])
                weights(f"XQ0_{i}")
            root_of_turn("NS0", n_root, TT)
            wait_read(act, "XS0")
            root(xs_b, xs_a)
            release(act.activation(r_row[:], ready("RB0"), ACT.Copy), "RB0")
            s = 0
            for c in range(TOKT // 2):
                for t in range(TT):
                    if s < CROSS_UNITS + 3:
                        cross_step(0, s)
                    s += 1
                    weights(f"V0_{c}_{t}")
            for t in range(TT):
                wait_read(act, f"V0_{TOKT // 2 - 1}_{t}")
                act.activation(v0[:, t, :], v0[:, t, :], ACT.Gelu).then_inc(v0_gelu, 1)
            act.wait_ge(ln_stats, 1)
            act.activation(ln_root, ln_mv.rearrange("p (t s) -> p t s", s=2)[:, :, 1], ACT.Sqrt,
                           bias=eps).then_inc(root_done, 1)

            def u_gelu(i):
                wait_read(act, f"U{i}")
                act.activation(u0[:, i, :], u0[:, i, :], ACT.Gelu).then_inc(u_done, 1)

            def gate_hi(i):
                act.wait_ge(gated_done, i + 1)
                act.activation(hid_hi[:, i, :], gated[:, i % 2, :], ACT.Copy).then_inc(hid_hi_done, 1)

            for i in range(TOKT):
                weights(f"U{i}")
                u_gelu(i)
                if i >= SPATIAL_LAG:
                    gate_hi(i - SPATIAL_LAG)
            for i in range(TOKT - SPATIAL_LAG, TOKT):
                gate_hi(i)

            for layer in range(DEPTH):
                if layer == 1:
                    for i in range(2):
                        q_evacuate(f"XQ1_{i}", qx[:, i, :], C_XQ[1], qx_sq[:, i, :])
                        weights(f"XQ1_{i}")
                    root_of_turn("NS2", n_root, TT)
                    act.wait_ge(n2_ready, 1)
                    for t in range(TT):
                        release(act.activation(v1[1][:, t, :], ready(f"V1_{t}")[:, 0:KVH * HD], ACT.Identity,
                                               scale=n_r[:, t:t + 1]), f"V1_{t}")
                        weights(f"V1_{t}")
                        if t == 0:
                            wait_read(act, "XS1")
                            root(xs_b, xs_a)
                    for t in range(TT):
                        wait_read(act, f"V1_{t}")
                    act.dma_start(v1[0][CHUNK:P, :, :], v1[1][0:CHUNK, :, :]).then_inc(v_shifted, 16)
                    act.dma_start(v1[0][0:CHUNK, 1:TT, :], v1[1][CHUNK:P, 0:TT - 1, :]).then_inc(v_shifted, 16)
                    cross_step(1, 0)

                    def swa_exp(w):
                        g, j = divmod(w, TT)
                        b = w % 2
                        act.wait_ge(neg_m_done, 2 * CROSS_UNITS + w + 1)
                        if w >= 2:
                            act.wait_ge(t_done, 2 * CROSS_UNITS + w - 1)
                        for e in range(4):
                            name = ("SA", "SB")[e // 2] + str(w)
                            c = j * HEADS + 4 * g + e
                            ins = act.activation(probs[:, b, e * P:(e + 1) * P],
                                                 acc_of(name)[:, (e % 2) * P:(e % 2 + 1) * P], ACT.Exp,
                                                 bias=neg_m[:, 4 * b + e:4 * b + e + 1], scale=qs_r[:, c:c + 1],
                                                 accum_out=sums[:, 4 * b + e:4 * b + e + 1])
                            if e % 2:
                                release(ins, name)
                        act.activation(sink_e[:, 4 * b:4 * b + 4], sink_d[:, 4 * b:4 * b + 4],
                                       ACT.Exp).then_inc(sink_exp, 1)

                    def swa_out(m):
                        g, jj = divmod(m, 2)
                        act.wait_ge(o_done, 2 * CROSS_UNITS + 2 * m + 2)
                        act.activation(
                            hid_hi[:, 2 * g:2 * g + 2, 2 * jj * P:(2 * jj + 2) * P].rearrange("p i (j t) -> p j i t", j=2),
                            swa_o(m).rearrange("p (j i t) -> p j i t", j=2, i=2), ACT.Copy).then_inc(hid_hi_done, 1)

                    def swa_step(w):
                        if w < SWA_UNITS:
                            swa_exp(w)
                        if w >= 4 and w % 2 == 0:
                            swa_out((w - 4) // 2)

                    def evacuate(kind, i):
                        if kind == "K":
                            q_evacuate(f"K{i}", key_tiles[i], C_BK, k_sq[:, i, :])
                        else:
                            act.wait_ge(turn_done, TURN[f"QN{i // 2 - 1}_1" if i >= 2 else "XS1"] + 1)
                            q_evacuate(f"Q{i}", q1[:, i, :], C_BQ, qx_sq[:, i % 2, :])
                        weights(f"{kind}{i}")

                    for n, tile in enumerate(KQ):
                        for part, todo in enumerate(STEPS_KQ[n]):
                            if part == 1:
                                evacuate(*tile)
                            for step, j in todo:
                                if step == "C":
                                    cross_step(1, j)
                                elif step == "S":
                                    swa_step(j)
                                elif step == "QN":
                                    wait_read(act, f"QN{j}_1")
                                    root(group(qs_b, j), group(qs_a, j))
                                elif step == "KC":
                                    act.wait_ge(keys_scaled, 2)
                                    act.dma_start(k1[HD:P, 0, :], k1[0:HD, 0, :]).then_inc(keys_copied, 16)
                                    act.dma_start(k1[0:HD, 1, :], k1[HD:P, 1, :]).then_inc(keys_copied, 16)
                                elif step == "KN":
                                    name = f"KN{j}_1"
                                    release(act.activation(k_sq[:, j, :], ready(name), ACT.Sqrt,
                                                           bias=cols[:, C_EPS_SQ:C_EPS_SQ + 1], scale=1.0 / HD), name)
                    for w in range(SWA_UNITS, SWA_STEPS):
                        swa_step(w)

                if layer == 1:
                    act.wait_ge(rotated, len(KQ))
                for d in range(KT):
                    weights(f"OUT{layer}_{d}")
                    wait_read(act, f"OUT{layer}_{d}")
                    prepare_hi(1 + 2 * layer, d, C_MLP[layer])
                if layer == 0:
                    act.dma_start(pos_i, pos.unsqueeze(0).broadcast_to([P, SEQ])).then_inc(pos_in, 16)
                for t in range(KT):
                    name = f"UP{layer}_0_{t}"
                    tn = TURN[name]
                    mlp_up(layer, 0, t, tn, bank(tn), tn // ACC + 1)
                    weights(name)
                body = TURN[f"DN{layer}_0_0"]
                hb = H_MLP[layer] + KT + SLOTS
                assert nexth[0] == hb
                with act.Fori(0, QUARTERS - 1) as q:
                    for j in range(2 * KT):
                        tn = q * (2 * KT) + (body + j)
                        if j < KT:
                            act.wait_ge(turn_done, tn + 1)
                        else:
                            mlp_up(layer, q + 1, j - KT, tn, bank(body + j),
                                   q * (2 * KT // ACC) + ((body + j) // ACC + 1))
                        h = hb + j
                        split_hi(h, q * (2 * KT // SLOTS * 16) + 16 * (h // SLOTS), h % SLOTS)
                nexth[0] = hb + 2 * KT * (QUARTERS - 1)
                if layer == 0:
                    for n, t in enumerate((sin_t, cos_t)):
                        act.wait_ge(sin_arg, n + 1)
                        act.activation(t, t, ACT.Sin).then_inc(trig_done, 1)
                for t in range(KT):
                    weights(f"DN{layer}_{QUARTERS - 1}_{t}")
                    if layer < DEPTH - 1:
                        act.wait_ge(x_updated, X_L * (layer + 1) - KT + t + 1)
                        prepare_hi(2 * (layer + 1), t, C_MIX[layer + 1])

        @block.vector
        def _(dve):
            steps = [0]

            def link(ins):
                steps[0] += 1
                ins.then_inc(dve_step, 1)
                dve.wait_ge(dve_step, steps[0])

            def ready(name):
                dve.wait_ge(turn_done, TURN[name] + 1)
                return acc_of(name)

            def along(ap, n):
                return ap.unsqueeze(2).broadcast_to([P, ap.shape[1], n])

            def prepare_lo(n, k, gain):
                dve.wait_ge(xg_hi_done, KT * n + k + 1)
                dve.scalar_tensor_tensor(xg_lo[:, k, :], x[:, k, :], cols[:, gain + k:gain + k + 1],
                                         xg_hi[:, k, :].bitcast(F32), ALU.mult,
                                         ALU.subtract).then_inc(xg_lo_done, 1)

            def norm_factors(name):
                wait_read(dve, name)
                link(dve.reciprocal(n_r, n_root))
                link(dve.tensor_tensor(n_r2, n_r, n_r, ALU.mult))

            def cross_factors(layer):
                name = f"XS{layer}"
                release(dve.tensor_tensor(v3(xs_a, TT), v3(ready(name)[:, 0:TT * XH], TT), along(n_r2, XH),
                                          ALU.mult), name)
                dve.wait_ge(root_done, ROOT[f"xs{layer}"])
                link(dve.reciprocal(xs_b, xs_b))
                link(dve.scalar_tensor_tensor(v3(xs_r, TT), v3(xs_b, TT), QK_SCALE, along(n_r, XH),
                                              ALU.mult, ALU.mult))

            def cross_max(layer, u):
                U = CROSS_UNITS * layer + u
                i, th, h2 = u // 4, (u // 2) % 2, u % 2
                b = U % 2
                dve.wait_ge(s_done, U + 1)
                link(dve.tensor_reduce(mx[:, 4 * b:4 * b + 2], v3(s_bank[:, h2, :], 2), AX, ALU.max))
                dve.scalar_tensor_tensor(neg_m[:, 4 * b:4 * b + 2], mx[:, 4 * b:4 * b + 2], -1.0,
                                         v3(xs_r, TT)[:, 2 * th:2 * th + 2, 2 * i + h2],
                                         ALU.mult, ALU.mult).then_inc(neg_m_done, 1)

            def cross_norm(layer, u):
                U = CROSS_UNITS * layer + u
                b = U % 2
                dve.wait_ge(exp_done, U + 1)
                link(dve.reciprocal(inv[:, 4 * b:4 * b + 2], sums[:, 4 * b:4 * b + 2]))
                dve.tensor_tensor(v3(probs[:, b, :], 2), v3(probs[:, b, :], 2), along(inv[:, 4 * b:4 * b + 2], MEM),
                                  ALU.mult).then_inc(pn_cross, 1)

            def cross_step(layer, s):
                if s < CROSS_UNITS:
                    cross_max(layer, s)
                if 1 <= s <= CROSS_UNITS:
                    cross_norm(layer, s - 1)
                if s == 6 or s == 10:
                    i = (s - 6) // 4
                    dve.wait_ge(hid_hi_done, HID_L * layer + i + 1)
                    dve.tensor_tensor(hid_lo[:, TOKT + i, :], o_bank[:], hid_hi[:, TOKT + i, :].bitcast(F32),
                                      ALU.subtract).then_inc(hid_done, 1)

            def out_update(layer, d):
                name = f"OUT{layer}_{d}"
                release(dve.tensor_tensor(x[:, d, :], ready(name), x[:, d, :], ALU.add), name)
                wait_read(dve, name)

            def mlp_up(layer, q, t, b, n_read):
                dve.wait_ge(acc_free[b], n_read)
                dve.wait_ge(hid_done, (q * KT) + (HID_L * layer + KT + t))
                dve.tensor_tensor(hid_sq, relu[:, t % 2, :], relu[:, t % 2, :], ALU.mult).then_inc(hid_squared, 1)
                dve.wait_ge(hid_squared, (q * KT) + (layer * QUARTERS * KT + t + 1))
                dve.wait_ge(hid_hi_done, (q * KT) + (HID_L * layer + KT + t + 1))
                dve.tensor_tensor(hid_lo[:, t, :], hid_sq, hid_hi[:, t, :].bitcast(F32),
                                  ALU.subtract).then_inc(hid_done, 1)

            def mlp_down(layer, q, t, tn, b, n_read):
                dve.wait_ge(turn_done, tn + 1)
                if t:
                    dve.wait_ge(x_updated, (q * KT) + (X_L * layer + t))
                dve.tensor_tensor(scaled, acc[:, b, :], r_row[:], ALU.mult).then_inc(acc_free[b], 1)
                dve.wait_ge(acc_free[b], n_read)
                dve.tensor_tensor(x[:, t, :], x[:, t, :], scaled, ALU.add).then_inc(x_updated, 1)
                if t == KT - 1:
                    dve.wait_ge(x_updated, (q * KT) + (X_L * layer + KT))

            def mem_split(l, k):
                gain = cols[:, C_MEM[l] + k:C_MEM[l] + k + 1]
                hi = hid_hi[:, k, l * MEM:(l + 1) * MEM]
                dve.wait_ge(mem_loaded[k // 2], 16)
                if l == 1:
                    link(dve.tensor_scalar(hi, mem_in[:, k, :], gain, None, ALU.mult))
                else:
                    dve.wait_ge(mem_hi, k + 1)
                dve.scalar_tensor_tensor(hid_lo[:, k, l * MEM:(l + 1) * MEM], mem_in[:, k, :], gain,
                                         hi.bitcast(F32), ALU.mult, ALU.subtract).then_inc(mem_lo, 1)

            def first_lo(part):
                ks = slice(part * KT // 2, (part + 1) * KT // 2)
                dve.wait_ge(w_hi_done if part else part_hi, 1)
                dve.tensor_tensor(w_lo[:, ks, slot(0)], w_raw[:, 0, :].rearrange("p (k n) -> p k n", k=KT)[:, ks, :],
                                  w_hi[:, ks, slot(0)].bitcast(F32), ALU.subtract).then_inc(w_ready if part else part_lo, 1)

            def split_lo(h):
                dve.wait_ge(w_hi_done, h + 1)
                dve.wait_ge(w_ready, h)
                dve.tensor_tensor(w_lo[:, :, slot(h)], w_raw[:, h % SLOTS, :].rearrange("p (k n) -> p k n", k=KT),
                                  w_hi[:, :, slot(h)].bitcast(F32), ALU.subtract).then_inc(w_ready, 1)

            first_lo(0)
            dve.wait_ge(cols_in, 16)
            for k in range(KT):
                mem_split(0, k)
                if k == 1:
                    first_lo(1)
            for k in range(KT):
                mem_split(1, k)
            n = KT // 2
            dve.wait_ge(memsq_done, 4)
            while n:
                ins = dve.tensor_tensor(mem_sq[:, 0:n, :], mem_sq[:, 0:n, :], mem_sq[:, n:2 * n, :], ALU.add)
                if n > 1:
                    link(ins)
                n //= 2
            ins.then_inc(memsq_added, 1)
            split_lo(5)
            for k in range(KT):
                prepare_lo(0, k, C_MIX[0])
                if k == KT // 2 - 1:
                    wait_read(dve, "MS")
                    link(dve.reciprocal(mem_r, mem_ms))
                    link(dve.tensor_copy(neg_sink, cols[:, C_SINK:C_SINK + HEADS]))
                    dve.tensor_scalar(neg_sink, neg_sink, -1.0, None, ALU.mult).then_inc(mem_r_ready, 1)

            def mem_key_scale(l):
                wait_read(dve, f"KN{l}")
                link(dve.reciprocal(k_sq0[:, l, :], k_sq0[:, l, :]))
                dve.tensor_tensor(kmem[:, l, :, :], kmem[:, l, :, :], v3(k_sq0[:, l, :], 2),
                                  ALU.mult).then_inc(kmem_done, 1)

            for k in range(KT):
                dve.wait_ge(x_squared, k + 1)
                if k:
                    dve.wait_ge(sq_added, k)
                    dve.tensor_tensor(sq_sum[:], sq_sum[:], x_sq[:, k % 2, :], ALU.add).then_inc(sq_added, 1)
                else:
                    dve.tensor_copy(sq_sum[:], x_sq[:, 0, :]).then_inc(sq_added, 1)
            for l in range(DEPTH):
                mem_key_scale(l)

            norm_factors("NS0")
            step = 0
            for c in range(TOKT // 2):
                for t in range(TT):
                    name = f"V0_{c}_{t}"
                    release(dve.tensor_scalar(v0[:, t, 2 * c * P:2 * (c + 1) * P], ready(name)[:, 0:2 * P],
                                              n_r[:, t:t + 1], None, ALU.mult), name)
                    if (c, t) == (0, 0):
                        dve.tensor_tensor(diag[:], ident.unsqueeze(1).broadcast_to([P, 4, P]), along(n_r, P),
                                          ALU.mult).then_inc(diag_done, 1)
                        cross_factors(0)
                    if step < CROSS_UNITS + 3:
                        cross_step(0, step)
                    step += 1
            for t in range(TT):
                dve.wait_ge(v0_gelu, t + 1)
                for e in range(2):
                    ins = dve.bn_stats(ln_st[:, 12 * t + 6 * e:12 * t + 6 * e + 6], v0[:, t, e * TOK // 2:(e + 1) * TOK // 2])
                link(ins)
                ins = dve.bn_aggr(ln_mv[:, 2 * t:2 * t + 2], ln_st[:, 12 * t:12 * t + 12])
            ins.then_inc(ln_stats, 1)
            dve.wait_ge(root_done, ROOT["ln"])
            link(dve.reciprocal(ln_r, ln_root))
            dve.wait_ge(ln_in, 48)
            dve.memset(wsT[CHUNK:P, :, 0:CHUNK], 0.0).then_inc(wsT_masked, 1)
            def u_scale(i):
                release(dve.tensor_tensor(u0[:, i, :], ready(f"U{i}"), r_row[:], ALU.mult), f"U{i}")

            wait_read(dve, "RB0")
            for t in range(TT):
                if t % 2 == 0:
                    u_scale(t // 2)
                link(dve.tensor_scalar(v0[:, t, :], v0[:, t, :], ln_mv[:, 2 * t:2 * t + 1], ln_r[:, t:t + 1],
                                       ALU.subtract, ALU.mult))
                ins = dve.tensor_tensor(v0[:, t, :], v0[:, t, :], ln_gb[:, 0, :], ALU.mult)
                if t < TT - 1:
                    ins.then_inc(v0_normed, 1)
                else:
                    link(ins)
                    dve.tensor_tensor(v0[:, t, :], v0[:, t, :], ln_gb[:, 1, :], ALU.add).then_inc(v0_done, 1)

            def sv_add(i):
                name = f"SV{i}"
                if i >= 2:
                    dve.wait_ge(hid_done, 2 + i - 1)
                release(dve.tensor_tensor(v3(gated[:, i % 2, :], TT), v3(ready(name), TT),
                                          bsx[:, i, :].unsqueeze(1).broadcast_to([P, TT, P]), ALU.add), name)

            def gate_lo(i):
                dve.wait_ge(hid_hi_done, 2 + i + 1)
                dve.tensor_tensor(hid_lo[:, i, :], gated[:, i % 2, :], hid_hi[:, i, :].bitcast(F32),
                                  ALU.subtract).then_inc(hid_done, 1)

            for i in range(TOKT):
                if i >= 2:
                    u_scale(i)
                if i >= SPATIAL_LAG + 2:
                    gate_lo(i - SPATIAL_LAG - 2)
                if i >= SPATIAL_LAG:
                    sv_add(i - SPATIAL_LAG)
            for i in range(TOKT - SPATIAL_LAG, TOKT):
                gate_lo(i - 2)
                sv_add(i)
            gate_lo(TOKT - 2)
            gate_lo(TOKT - 1)

            def round_of(out_, in_, scale):
                link(dve.tensor_scalar(out_, in_, scale, ROUND, ALU.mult, ALU.add))
                link(dve.tensor_scalar(out_, out_, -ROUND, None, ALU.add))

            def less(a, n, c):
                link(dve.scalar_tensor_tensor(a, n, -c, a, ALU.mult, ALU.add))

            def rotation_angles(step):
                if step == 0:
                    dve.wait_ge(pos_in, 16)
                    link(dve.tensor_scalar(ang, pos_i, cols[:, C_FREQ:C_FREQ + 1], None, ALU.mult))
                    round_of(turns_n, ang, 1.0 / FAR)
                elif step == 1:
                    less(ang, turns_n, FAR_1)
                    less(ang, turns_n, FAR_2)
                    link(dve.tensor_scalar(far_t, turns_n, FAR_3, None, ALU.mult))
                elif step in (2, 4):
                    round_of(turns_n, ang, 1.0 / TWO_PI)
                elif step in (3, 5):
                    less(ang, turns_n, PI_1)
                    less(ang, turns_n, PI_2)
                    less(ang, turns_n, PI_3)
                    if step == 3:
                        link(dve.tensor_tensor(ang, ang, far_t, ALU.subtract))
                else:
                    link(dve.tensor_scalar(sin_t, ang, BELOW_PI, -BELOW_PI, ALU.min, ALU.max))
                    link(dve.scalar_tensor_tensor(far_t, sin_t, -1.0, sin_t, ALU.mult, ALU.max))
                    dve.tensor_scalar(cos_t, far_t, -1.0, np.pi / 2, ALU.mult, ALU.add).then_inc(sin_arg, 2)

            for layer in range(DEPTH):
                if layer == 1:
                    norm_factors("NS2")
                    dve.wait_ge(sq_added, 3 * KT)
                    for b in swapped:
                        dve.memset(b, 0.0).then_inc(swap_zeroed, 1)
                    dve.tensor_copy(scaled_mx, n_r).then_inc(n2_ready, 1)
                    cross_factors(1)
                    dve.memset(v1[0][0:CHUNK, 0, :], 0.0).then_inc(v_zeroed, 1)
                    cross_step(1, 0)
                    dve.wait_ge(trig_done, 2)

                    def rotate_tile(tile, n):
                        b = swapped[n % 4]
                        dve.wait_ge(swap_in[n % 4], 64 * (n // 4 + 1))
                        link(dve.tensor_tensor(b, b, sin_t, ALU.mult))
                        dve.wait_ge(rot_cos, n + 1)
                        dve.tensor_tensor(tile, tile, b, ALU.add).then_inc(rotated, 1)

                    def key_reciprocal(g, half):
                        wait_read(dve, f"KN{g}_1")
                        a = k_sq[:, g, half * SEQ // 2:(half + 1) * SEQ // 2]
                        link(dve.reciprocal(a, a))

                    def key_scale(n):
                        key_reciprocal(n, 1)
                        dve.wait_ge(rotated, KQ.index(("K", n)) + 1)
                        for g, po in ((0, slice(0, HD)), (1, slice(HD, P))) if n == 0 else ((2, slice(0, P)),):
                            dve.tensor_tensor(k1[po, g, :], key_tiles[n][po, :], k_sq[po, n, :],
                                              ALU.mult).then_inc(keys_scaled, 1)

                    def query_squares(g):
                        name = f"QN{g}_1"
                        release(dve.tensor_tensor(group(qs_a, g), v3(ready(name)[:, 0:TT * 4], TT), along(n_r2, 4),
                                                  ALU.mult), name)

                    def query_factors(g):
                        dve.wait_ge(root_done, ROOT[f"qs{g}"])
                        link(dve.reciprocal(group(qs_b, g), group(qs_b, g)))
                        link(dve.scalar_tensor_tensor(group(qs_r, g), group(qs_b, g), QK_SCALE, along(n_r, 4),
                                                      ALU.mult, ALU.mult))

                    def swa_max(w):
                        g, j = divmod(w, TT)
                        b = w % 2
                        m = mx[:, 4 * b:4 * b + 4]
                        banks = [v3(ready(f"S{e}{w}")[:, 0:2 * P], 2) for e in "AB"]
                        if j == 0:
                            for s in banks:
                                ins = dve.memset(s[0:CHUNK, :, 0:CHUNK], NO_KEY)
                            link(ins)
                        for e, s in enumerate(banks):
                            ins = dve.tensor_reduce(m[:, 2 * e:2 * e + 2], s, AX, ALU.max)
                        link(ins)
                        link(dve.tensor_tensor(scaled_mx, m, v3(qs_r, TT)[:, j, 4 * g:4 * g + 4], ALU.mult))
                        nm = neg_m[:, 4 * b:4 * b + 4]
                        link(dve.scalar_tensor_tensor(nm, scaled_mx, -1.0, neg_sink[:, 4 * g:4 * g + 4],
                                                      ALU.mult, ALU.min))
                        dve.tensor_tensor(sink_d[:, 4 * b:4 * b + 4], nm,
                                          cols[:, C_SINK + 4 * g:C_SINK + 4 * g + 4], ALU.add).then_inc(neg_m_done, 1)

                    def swa_inverse(w):
                        b = w % 2
                        wait_read(dve, f"SB{w}")
                        dve.wait_ge(sink_exp, w + 1)
                        if w:
                            dve.wait_ge(inv_done, w)
                        link(dve.tensor_tensor(tot, sums[:, 4 * b:4 * b + 4], sink_e[:, 4 * b:4 * b + 4], ALU.add))
                        if w >= 2:
                            dve.wait_ge(pn_swa, w - 1)
                        dve.reciprocal(inv[:, 4 * b:4 * b + 4], tot).then_inc(inv_done, 1)

                    def swa_pT(w):
                        U = 2 * CROSS_UNITS + w
                        dve.wait_ge(t_done, U + 1)
                        dve.wait_ge(o_done, U - 1)
                        dve.tensor_copy(probsT[:, w % 2, :], swa_t(w)).then_inc(pT_dve, 1)

                    def swa_out(m):
                        g, jj = divmod(m, 2)
                        dve.wait_ge(hid_hi_done, HID_L + 2 + m + 1)

                        def part(a):
                            return a[:, 2 * g:2 * g + 2, 2 * jj * P:(2 * jj + 2) * P].rearrange(
                                "p i (j t) -> p j i t", j=2)
                        dve.tensor_tensor(part(hid_lo), swa_o(m).rearrange("p (j i t) -> p j i t", j=2, i=2),
                                          part(hid_hi).bitcast(F32), ALU.subtract).then_inc(hid_done, 1)

                    def swa_step(w):
                        if w % TT == 0 and w < SWA_UNITS:
                            query_factors(w // TT)
                        if w < SWA_UNITS:
                            swa_max(w)
                        if 1 <= w <= SWA_UNITS:
                            swa_inverse(w - 1)
                        if 2 <= w < SWA_UNITS + 2:
                            swa_pT(w - 2)
                        if w >= 4 and w % 2 == 0:
                            swa_out((w - 4) // 2)

                    for n, (kind, i) in enumerate(KQ):
                        for part, todo in enumerate(STEPS_KQ[n]):
                            if part == 1:
                                if 1 <= n < len(KQ) - 1:
                                    rotate_tile(kq_tiles[n - 1], n - 1)
                            for step, j in todo:
                                if step == "C":
                                    cross_step(1, j)
                                elif step == "S":
                                    swa_step(j)
                                elif step == "QN":
                                    query_squares(j)
                                elif step == "KR":
                                    key_reciprocal(j, 0)
                                elif step == "KS":
                                    key_scale(j)
                                if (step, j) in (("S", 4), ("S", 5)):
                                    rotate_tile(kq_tiles[j - 6], len(KQ) + j - 6)
                    for w in range(SWA_UNITS, SWA_STEPS):
                        swa_step(w)

                for d in range(KT):
                    out_update(layer, d)
                    if d >= 1:
                        prepare_lo(1 + 2 * layer, d - 1, C_MLP[layer])
                prepare_lo(1 + 2 * layer, KT - 1, C_MLP[layer])
                for t in range(KT):
                    tn = TURN[f"UP{layer}_0_{t}"]
                    mlp_up(layer, 0, t, bank(tn), tn // ACC + 1)
                    if t == 1:
                        name = f"NS{1 + 2 * layer}"
                        release(dve.tensor_scalar(r_row[:], ready(name), 1.0 / D, EPS, ALU.mult, ALU.add), name)
                        wait_read(dve, name)
                    if t in (2, 4, 6, 7):
                        n = (2, 4, 6, 7).index(t)
                        ins = dve.reciprocal(r_row[:, n * P:(n + 1) * P], r_row[:, n * P:(n + 1) * P])
                        if n == 3:
                            link(ins)
                    if layer == 0 and t >= 1:
                        rotation_angles(t - 1)
                body = TURN[f"DN{layer}_0_0"]
                with dve.Fori(0, QUARTERS - 1) as q:
                    for j in range(2 * KT):
                        n_read = q * (2 * KT // ACC) + ((body + j) // ACC + 1)
                        if j < KT:
                            mlp_down(layer, q, j, q * (2 * KT) + (body + j), bank(body + j), n_read)
                        else:
                            mlp_up(layer, q + 1, j - KT, bank(body + j), n_read)
                for t in range(KT):
                    tn = TURN[f"DN{layer}_{QUARTERS - 1}_{t}"]
                    mlp_down(layer, QUARTERS - 1, t, tn, bank(tn), tn // ACC + 1)
                    if layer < DEPTH - 1 and t >= 1:
                        prepare_lo(2 * (layer + 1), t - 1, C_MIX[layer + 1])
                if layer < DEPTH - 1:
                    prepare_lo(2 * (layer + 1), KT - 1, C_MIX[layer + 1])

        @block.tensor
        def _(pe):
            def open_turn(name):
                t = TURN[name]
                if t >= ACC:
                    pe.wait_ge(acc_free[bank(t)], t // ACC)
                return acc_of(name)

            def close(ins):
                ins.then_inc(turn_done, 1)

            def split_product(out_, st, mv, start, stop):
                pe.matmul(out_, st[0], mv[0], start=start, stop=False)
                pe.matmul(out_, st[0], mv[1], start=False, stop=False)
                return pe.matmul(out_, st[1], mv[0], start=False, stop=stop)

            def weight(h, k, n=1, width=None):
                s = slot(h, n)
                s = slice(s.start, s.start + width) if width else s
                return w_hi[:, k, s], w_lo[:, k, s]

            def both(hi, lo, k, s):
                return hi[:, k, s], lo[:, k, s]

            ALL = slice(0, SEQ)

            def project(out_, h, hi, lo, order=range(KT), before=None, start=True, stop=True, s=ALL):
                order = list(order)
                for k in order:
                    if before:
                        before(k)
                    ins = split_product(out_, weight(h, k), both(hi, lo, k, s), start and k == order[0],
                                        stop and k == order[-1])
                return ins

            def project_x(name, h, norm=None):
                out_ = open_turn(name)
                pe.wait_ge(w_ready, h + 1)
                close(project(out_, h, xg_hi, xg_lo, before=None if norm is None else
                              lambda k: pe.wait_ge(xg_lo_done, KT * norm + k + 1)))

            def project_tokens(name, h, t, width):
                out_ = open_turn(name)
                pe.wait_ge(w_ready, h + 2)
                for k in range(KT):
                    xs = both(xg_hi, xg_lo, k, slice(t * P, (t + 1) * P))
                    ins = split_product(out_[:, 0:width], xs, weight(h, k, 2, width), k == 0, k == KT - 1)
                close(ins)

            def norm_sums(n):
                out_ = open_turn(f"NS{n}")
                pe.wait_ge(sq_added, KT * (n + 1))
                for t in range(TT):
                    ins = pe.matmul(out_[:, t:t + 1], sq_sum[:, t * P:(t + 1) * P], ones[:, 0:1], start=True, stop=True)
                close(ins)

            def cross_squares(layer):
                wait_read(pe, f"XQ{layer}_0")
                wait_read(pe, f"XQ{layer}_1")
                out_ = open_turn(f"XS{layer}")
                for i in range(2):
                    for t in range(TT):
                        c = t * XH + 2 * i
                        ins = pe.matmul(out_[:, c:c + 2], qx_sq[:, i, t * P:(t + 1) * P], blocks, start=True, stop=True)
                close(ins)

            def cross_scores(layer, u):
                U = CROSS_UNITS * layer + u
                i, th, h2 = u // 4, (u // 2) % 2, u % 2
                po = slice(h2 * HD, (h2 + 1) * HD)
                if u == 0:
                    pe.wait_ge(kmem_done, layer + 1)
                if U >= 2:
                    pe.wait_ge(exp_done, U - 1)
                for t2 in range(2):
                    t = 2 * th + t2
                    ins = pe.matmul(s_bank[:, h2, t2 * MEM:(t2 + 1) * MEM], qx[po, i, t * P:(t + 1) * P],
                                    kmem[po, layer, i, :], start=True, stop=True)
                ins.then_inc(s_done, 1)

            def cross_transpose(layer, u):
                U = CROSS_UNITS * layer + u
                pe.wait_ge(pn_cross, U + 1)
                if U:
                    pe.wait_ge(pT_act, U)
                for m in range(MT):
                    for t2 in range(2):
                        c = t2 * MEM + m * P
                        ins = pe.transpose(t_bank[:, (2 * m + t2) * P:(2 * m + t2 + 1) * P],
                                           probs[:, U % 2, c:c + P], ident)
                ins.then_inc(t_done, 1)

            def cross_values(layer, u):
                U = CROSS_UNITS * layer + u
                i, th, h2 = u // 4, (u // 2) % 2, u % 2
                h = 2 * i + h2
                pe.wait_ge(pT_act, U + 1)
                if u % 4 == 0 and U:
                    pe.wait_ge(hid_done, HID_L * layer + 1 if u else hid_after(layer - 1))
                for m in range(MT):
                    ins = pe.matmul(o_bank[h2 * HD:(h2 + 1) * HD, th * 2 * P:(th + 1) * 2 * P],
                                    vmem[:, layer, m, h * HD:(h + 1) * HD],
                                    probsT[:, U % 2, m * 2 * P:(m + 1) * 2 * P], start=(m == 0), stop=(m == MT - 1))
                ins.then_inc(o_done, 1)

            def hid_after(layer):
                return HID_L * (layer + 1)

            def cross_step(layer, s):
                if s < CROSS_UNITS:
                    cross_scores(layer, s)
                if 2 <= s < CROSS_UNITS + 2:
                    cross_transpose(layer, s - 2)
                if 3 <= s < CROSS_UNITS + 3:
                    cross_values(layer, s - 3)

            def up(layer, q, t, h, w_count, free, norm=None):
                b = bank(TURN[f"UP{layer}_{q}_{t}"])
                pe.wait_ge(acc_free[b], free)
                pe.wait_ge(w_ready, w_count)
                close(project(acc[:, b, :], h, xg_hi, xg_lo, before=None if norm is None else
                              lambda k: pe.wait_ge(xg_lo_done, KT * norm + k + 1)))

            def down(layer, t, h, w_count, b, free, hid_base):
                pe.wait_ge(acc_free[b], free)
                pe.wait_ge(w_ready, w_count)
                close(project(acc[:, b, :], h, hid_hi, hid_lo,
                              before=(lambda k: pe.wait_ge(hid_done, hid_base + (k + 1))) if t == 0 else None))

            pe.wait_ge(ones_set, 1)
            for i in range(WARM_UP):
                pe.matmul(acc[:, ACC - 1, 0:P], ones[:], ones[:], start=True, stop=True)

            def mem_ready(h, l, k):
                if h == 0 and k == 0:
                    pe.wait_ge(part_lo, 1)
                if h == 0 and k == KT // 2:
                    pe.wait_ge(w_ready, 1)
                pe.wait_ge(mem_lo, KT * l + k + 1)

            def mem_keys(l):
                out_ = open_turn(f"MK{l}")
                for i in range(2):
                    h = H_MEMK[l] + i
                    if h:
                        pe.wait_ge(w_ready, h + 1)
                    ins = project(out_[:, i * MEM:(i + 1) * MEM], h, hid_hi, hid_lo, s=slice(l * MEM, (l + 1) * MEM),
                                  before=lambda k: mem_ready(h, l, k))
                close(ins)

            for l in range(DEPTH):
                mem_keys(l)

            def mem_values(l):
                out_ = open_turn(f"MV{l}")
                h = H_MEMV[l]
                pe.wait_ge(w_ready, h + 2)
                for m in range(MT):
                    for k in range(KT):
                        s = slice(l * MEM + m * P, l * MEM + (m + 1) * P)
                        ins = split_product(out_[:, m * XW:(m + 1) * XW], both(hid_hi, hid_lo, k, s),
                                            weight(h, k, 2), k == 0, k == KT - 1)
                close(ins)

            out_ = open_turn("MS")
            pe.wait_ge(ones_set, 1)
            pe.wait_ge(memsq_added, 1)
            for m in range(MT):
                ins = pe.matmul(out_[:, m:m + 1], mem_sq[:, 0, m * P:(m + 1) * P], ones[:, 0:1], start=True, stop=True)
            close(ins)
            mem_values(0)
            pe.wait_ge(tabs_in, 16)
            pe.wait_ge(eps_set, 1)
            for l in range(DEPTH):
                out_ = open_turn(f"KN{l}")
                wait_read(pe, f"MK{l}")
                pe.matmul(out_, same_head, k_sq0[:, l, :], start=True, stop=False)
                close(pe.matmul(out_, eps_share[:], mem_sq[:, 0:1, :].broadcast_to([P, 2, MEM]), start=False, stop=True))
            mem_values(1)

            project_x("XQ0_0", H_XQ[0], norm=0)
            project_x("XQ0_1", H_XQ[0] + 1)
            norm_sums(0)
            step = 0
            for c in range(TOKT // 2):
                for t in range(TT):
                    project_tokens(f"V0_{c}_{t}", H_V0 + 2 * c, t, 2 * P)
                    if (c, t) == (0, 0):
                        cross_squares(0)
                        out_ = open_turn("RB0")
                        pe.wait_ge(diag_done, 1)
                        close(pe.matmul(out_, ones[:], diag.rearrange("p a b -> p (a b)"), start=True, stop=True))
                    if step < CROSS_UNITS + 3:
                        cross_step(0, step)
                    step += 1

            def spatial(i):
                out_ = open_turn(f"SV{i}")
                pe.wait_ge(v0_done, TT)
                pe.wait_ge(wsT_masked, 1)
                lo, hi = i * P // GC, ((i + 1) * P - 1) // GC
                for n in range(TT):
                    for g in range(lo, hi + 1):
                        a, z = max(g * GC, i * P), min((g + 1) * GC, (i + 1) * P)
                        ins = pe.matmul(out_[a - i * P:z - i * P, n * P:(n + 1) * P], v0[:, n, a:z], wsT[:, g, :],
                                        start=True, stop=True)
                close(ins)

            for i in range(TOKT):
                project_x(f"U{i}", H_U0 + i)
                if i >= SPATIAL_LAG:
                    spatial(i - SPATIAL_LAG)
            for i in range(TOKT - SPATIAL_LAG, TOKT):
                spatial(i)

            for layer in range(DEPTH):
                if layer == 1:
                    project_x("XQ1_0", H_XQ[1], norm=2)
                    project_x("XQ1_1", H_XQ[1] + 1)
                    norm_sums(2)
                    for t in range(TT):
                        project_tokens(f"V1_{t}", H_V1, t, KVH * HD)
                        if t == 0:
                            cross_squares(1)
                    cross_step(1, 0)

                    def key_norm(n):
                        out_ = open_turn(f"KN{n}_1")
                        wait_read(pe, f"K{n}")
                        pe.matmul(out_, same_head, k_sq[:, n, :], start=True, stop=False)
                        close(pe.matmul(out_, eps_share[:], sq_sum[:], start=False, stop=True))

                    def query_norm(g):
                        out_ = open_turn(f"QN{g}_1")
                        for i in range(2):
                            wait_read(pe, f"Q{2 * g + i}")
                            for t in range(TT):
                                ins = pe.matmul(v3(out_[:, 4 * t:4 * t + 4], 2)[:, :, i],
                                                qx_sq[:, i, t * P:(t + 1) * P], blocks, start=True, stop=True)
                        close(ins)

                    def swa_scores(w):
                        g, j = divmod(w, TT)
                        if j == 0:
                            if g < 2:
                                pe.wait_ge(keys_copied, 32)
                            else:
                                pe.wait_ge(keys_scaled, 3)
                            pe.wait_ge(rotated, KQ.index(("Q", 2 * g + 1)) + 1)
                        for e in range(2):
                            out_ = open_turn(f"S{'AB'[e]}{w}")
                            po = slice(e * HD, (e + 1) * HD)
                            for c in range(2):
                                for i in range(2):
                                    first = j * P + (c - 1) * CHUNK
                                    skip = max(0, -first)
                                    ins = pe.matmul(out_[c * CHUNK:(c + 1) * CHUNK, i * P + skip:(i + 1) * P],
                                                    q1[po, 2 * g + i, j * P + c * CHUNK:j * P + (c + 1) * CHUNK],
                                                    k1[po, g, first + skip:first + P], start=True, stop=True)
                            close(ins)

                    def swa_transpose(w):
                        pe.wait_ge(pn_swa, w + 1)
                        if w >= 2:
                            pe.wait_ge(pT_dve, w - 1)
                        else:
                            pe.wait_ge(pT_act, 2 * CROSS_UNITS)
                            pe.wait_ge(exp_done, 2 * CROSS_UNITS)
                        for e in range(4):
                            ins = pe.transpose(swa_t(w)[:, e * P:(e + 1) * P], probs[:, w % 2, e * P:(e + 1) * P], ident)
                        ins.then_inc(t_done, 1)

                    def swa_values(w):
                        g, j = divmod(w, TT)
                        m, jj = divmod(w, 2)
                        if jj == 0:
                            pe.wait_ge(hid_done, HID_L + 2 + max(0, m - 1))
                        if w == 0:
                            pe.wait_ge(v_shifted, 32)
                            pe.wait_ge(v_zeroed, 1)
                            for t in range(TT):
                                wait_read(pe, f"V1_{t}")
                        pe.wait_ge(pT_dve, w + 1)
                        o = swa_o(m).rearrange("p (j i t) -> p j i t", j=2, i=2)
                        pT = v3(probsT[:, w % 2, :], 4)
                        for e in range(2):
                            for c in range(2):
                                cs = slice(c * CHUNK, (c + 1) * CHUNK)
                                ins = pe.matmul(o[e * HD:(e + 1) * HD, jj, :, cs], v1[c][:, j, g * HD:(g + 1) * HD],
                                                pT[:, 2 * e:2 * e + 2, cs], start=True, stop=True)
                        ins.then_inc(o_done, 1)

                    def swa_step(w):
                        if w < SWA_UNITS:
                            swa_scores(w)
                        if 2 <= w < SWA_UNITS + 2:
                            swa_transpose(w - 2)
                        if w >= 3:
                            swa_values(w - 3)

                    do = {"C": lambda j: cross_step(1, j), "S": swa_step, "KN": key_norm, "QN": query_norm}
                    for n, (kind, i) in enumerate(KQ):
                        h = H_KQ + n
                        out_ = open_turn(f"{kind}{i}")
                        pe.wait_ge(w_ready, h + 1)
                        for part, todo in enumerate(STEPS_KQ[n]):
                            ks = range(part * KT // 2, (part + 1) * KT // 2)
                            ins = project(out_, h, xg_hi, xg_lo, ks, start=part == 0, stop=part == 1)
                            if part == 1:
                                close(ins)
                            for step, j in todo:
                                if step in do:
                                    do[step](j)

                h = H_OUT[layer]
                mixed = HID_L * layer
                if layer == 0:
                    ready_at = {6: 1, 7: 2} | {i: 3 + i for i in range(TOKT)}
                else:
                    ready_at = {6: 1, 7: 2} | {i: 4 + 2 * (i // 2) for i in range(TOKT)}

                def heads_ready(k):
                    pe.wait_ge(hid_done, mixed + ready_at[k])

                late = 2
                order = [6, 7, *range(TOKT)]
                outs = []
                for d in range(SLOTS):
                    outs.append(open_turn(f"OUT{layer}_{d}"))
                    pe.wait_ge(w_ready, h + d + 1)
                    project(outs[d], h + d, hid_hi, hid_lo, order[:-late], heads_ready if d == 0 else None, stop=False)
                    if layer == 1 and d < SWA_STEPS - SWA_UNITS:
                        swa_step(SWA_UNITS + d)
                for d in range(SLOTS):
                    close(project(outs[d], h + d, hid_hi, hid_lo, order[-late:], heads_ready if d == 0 else None,
                                  start=False))
                for d in range(SLOTS, KT):
                    out_ = open_turn(f"OUT{layer}_{d}")
                    pe.wait_ge(w_ready, h + d + 1)
                    close(project(out_, h + d, hid_hi, hid_lo))

                n = 1 + 2 * layer
                for t in range(KT):
                    tn = TURN[f"UP{layer}_0_{t}"]
                    up(layer, 0, t, H_MLP[layer] + t, H_MLP[layer] + t + 1, tn // ACC, n if t == 0 else None)
                    if t == 1:
                        pe.wait_ge(sq_added, KT * (n + 1))
                        close(pe.matmul(open_turn(f"NS{n}"), ones[:], sq_sum[:], start=True, stop=True))
                body = TURN[f"DN{layer}_0_0"]
                hb = H_MLP[layer] + KT
                hid0 = HID_L * layer + KT
                with pe.Fori(0, QUARTERS - 1) as q:
                    for j in range(2 * KT):
                        w_count = q * (2 * KT) + (hb + j + 1)
                        free = q * (2 * KT // ACC) + ((body + j) // ACC)
                        if j < KT:
                            down(layer, j, hb + j, w_count, bank(body + j), free, q * KT + hid0)
                        else:
                            up(layer, 1, j - KT, hb + j, w_count, free)
                hb += 2 * KT * (QUARTERS - 1)
                for t in range(KT):
                    tn = TURN[f"DN{layer}_{QUARTERS - 1}_{t}"]
                    down(layer, t, hb + t, hb + t + 1, bank(tn), tn // ACC, hid0 + (QUARTERS - 1) * KT)


def tiled(a):
    return a.reshape(-1, P, a.shape[-1]).transpose(1, 0, 2)


def weight_halves(w):
    return tiled(w).reshape(P, KT, -1, P).transpose(2, 0, 1, 3).reshape(-1, P, KT * P)


def lay_out(a):
    f = np.float32
    w = []

    def add(m):
        w.append(weight_halves(m))

    for l in range(DEPTH):
        add(a["w_mem_kv"][l][:, :XW])
    for l in range(DEPTH):
        add(a["w_mem_kv"][l][:, XW:])
    ain, bin_ = a["a_w_in"][0], a["b_w_in"][0]
    kv = KVH * HD
    for l, w_out in ((0, a["a_w_out"][0]), (1, a["b_w_out"][0])):
        if l == 0:
            add(ain[:, 2 * TOK:])
            add(ain[:, TOK:2 * TOK])
            add(ain[:, :TOK])
        else:
            add(bin_[:, TOK + 2 * kv:])
            add(np.concatenate([bin_[:, TOK + kv:TOK + 2 * kv], np.zeros((D, 2 * P - kv), f)], 1))
            for kind, i in KQ:
                if kind == "K":
                    k = [bin_[:, TOK + g * HD:TOK + (g + 1) * HD] for g in ((0, 1), (2, 2))[i]]
                    add(np.concatenate(k, 1))
                else:
                    add(bin_[:, i * P:(i + 1) * P])
        add(w_out)
        for q in range(QUARTERS):
            add(a["w_up"][l][:, q * D:(q + 1) * D])
            add(a["w_down"][l][q * D:(q + 1) * D])
    halves = np.concatenate(w, 0)
    halves = np.concatenate([halves, np.zeros((2 * PAIRS - HALVES, P, KT * P), f)], 0)
    weights = halves.reshape(PAIRS, 2, P, KT * P).transpose(0, 2, 1, 3).reshape(PAIRS, P, 2 * KT * P)

    cols = np.zeros((P, N_COLS), f)
    for l in range(DEPTH):
        for at, name in ((C_MIX, "ln_mix"), (C_MLP, "ln_mlp"), (C_MEM, "ln_mem")):
            cols[:, at[l]:at[l] + KT] = a[name][l].reshape(KT, P).T
        cols[:, C_XQ[l]] = np.tile(a["xq_norm"][l], 2)
        cols[:, C_XK[l]] = np.tile(a["xk_norm"][l], 2)
    cols[:, C_BQ] = np.tile(a["b_q_norm"][0], 2)
    cols[:, C_BK] = np.tile(a["b_k_norm"][0], 2)
    half = ROPE_DIM // 2
    freq = np.power(f(ROPE_THETA), -np.arange(0, ROPE_DIM, 2, dtype=f) / f(ROPE_DIM))
    for p in range(P):
        if p % HD < ROPE_DIM:
            cols[p, C_FREQ] = freq[p % HD % half] * (-1 if p % HD < half else 1)
    cols[:, C_EPS] = EPS
    cols[:, C_EPS_SQ] = EPS * EPS
    cols[:, C_SINK:] = a["b_sinks"][0].reshape(KVH, 2, 2).transpose(0, 2, 1).reshape(1, HEADS)

    tabs = np.zeros((P, 2, P), f)
    tabs[:, 0] = np.eye(P, dtype=f)
    for p in range(P):
        tabs[p, 1, p // HD * HD:(p // HD + 1) * HD] = 1.0
    channel_group = np.arange(TOK) // GC
    bsx = a["a_b_s"][0][channel_group].reshape(TOKT, P, P).transpose(1, 0, 2)
    return {
        "xT": tiled(a["x"][0].T), "memT": tiled(a["mem"][0].T), "pos": a["positions"][0], "W": weights,
        "cols_d": cols, "tabs_d": tabs, "ln_d": np.stack([a["a_ln_g"][0], a["a_ln_b"][0]]), "bsx_d": bsx,
        "wsT_d": a["a_w_s"][0].transpose(2, 0, 1),
    }


def kernel(**inputs):
    import concourse.bacc as bacc
    from concourse.bass_utils import run_bass_kernel_spmd

    laid = lay_out({k: np.asarray(v) for k, v in inputs.items()})
    nc = bacc.Bacc("TRN2", target_bir_lowering=False, num_devices=1)
    arrays, args = {}, {}
    for name, a in laid.items():
        a = np.ascontiguousarray(a)
        arrays[f"in_{name}"] = a
        args[name] = nc.dram_tensor(f"in_{name}", a.shape, mybir.dt.from_np(a.dtype), kind="ExternalInput").ap()
    args["out"] = nc.dram_tensor("out_T", (P, KT, SEQ), F32, kind="ExternalOutput").ap()
    build(nc, **args)
    r = run_bass_kernel_spmd(nc, [arrays], core_ids=[0])
    o = r.results[0]["out_T"]
    return o.transpose(1, 0, 2).reshape(D, SEQ).T[None]
```
